# Optimizing a Trainium2 kernel written in Bass

```python
import math
import jax, jax.numpy as jnp
from jax import lax
import numpy as np

D_MODEL = 1024
BATCH = 1
SEQ = 2048
DEPTH = 1

CHUNK = 64
PLE_DIM = 256
CONV_DIM = 512
CONV_WIDTH = 31
N_HEADS = 8
N_KV_HEADS = 2
HEAD_DIM = 64
ATTN_DIM = N_HEADS * HEAD_DIM
KV_DIM = N_KV_HEADS * HEAD_DIM
GROUP = N_HEADS // N_KV_HEADS
WINDOW = 128
WINDOW_CHUNKS = WINDOW // CHUNK
ROPE_THETA = 10000.0
D_FF = 2816
FFN_CONV_WIDTH = 3
N_BRANCHES = 2
EPS = 1e-6
IN_DIM = 2 * CONV_DIM + ATTN_DIM + 2 * KV_DIM + N_BRANCHES * D_MODEL

kernel_name = "hybrid_conformer_swa_sink_gated_block"

def rms_norm(x, g):
    xf = x.astype(jnp.float32)
    y = xf * lax.rsqrt(jnp.mean(xf * xf, axis=-1, keepdims=True) + EPS)
    return (y * g.astype(jnp.float32)).astype(x.dtype)

def layer_norm(x, g, b):
    xf = x.astype(jnp.float32)
    mu = jnp.mean(xf, axis=-1, keepdims=True)
    var = jnp.mean(jnp.square(xf - mu), axis=-1, keepdims=True)
    y = (xf - mu) * lax.rsqrt(var + EPS)
    return (y * g.astype(jnp.float32) + b.astype(jnp.float32)).astype(x.dtype)

def causal_depthwise_conv(x, w, b):
    K, C = w.shape
    y = lax.conv_general_dilated(
        x, w[:, None, :].astype(x.dtype), window_strides=(1,), padding=[(K - 1, 0)],
        dimension_numbers=('NWC', 'WIO', 'NWC'), feature_group_count=C)
    return y + b.astype(x.dtype)

def apply_rope(t, positions):
    half = HEAD_DIM // 2
    inv_freq = ROPE_THETA ** (-jnp.arange(half, dtype=jnp.float32) / half)
    ang = positions.astype(jnp.float32)[..., None] * inv_freq
    cos = jnp.cos(ang)[:, :, None, :]
    sin = jnp.sin(ang)[:, :, None, :]
    tf = t.astype(jnp.float32)
    t1, t2 = tf[..., :half], tf[..., half:]
    return jnp.concatenate([t1 * cos - t2 * sin, t2 * cos + t1 * sin], axis=-1).astype(t.dtype)

def sliding_window_sink_attention(q, k, v, sinks):
    B, S = q.shape[0], q.shape[1]
    nc = S // CHUNK
    qc = q.reshape(B, nc, CHUNK, N_KV_HEADS, GROUP, HEAD_DIM)
    kc = k.reshape(B, nc, CHUNK, N_KV_HEADS, HEAD_DIM)
    vc = v.reshape(B, nc, CHUNK, N_KV_HEADS, HEAD_DIM)

    def band(t):
        pad = jnp.zeros_like(t[:, :WINDOW_CHUNKS - 1])
        tp = jnp.concatenate([pad, t], axis=1)
        return jnp.concatenate([tp[:, j:j + nc] for j in range(WINDOW_CHUNKS)], axis=2)

    kb, vb = band(kc), band(vc)
    scale = HEAD_DIM ** -0.5
    scores = jnp.einsum('bnqhgd,bnkhd->bnhgqk', qc, kb,
                        preferred_element_type=jnp.float32) * scale
    key_chunk = (jnp.arange(nc)[:, None] - (WINDOW_CHUNKS - 1)
                 + jnp.arange(WINDOW)[None, :] // CHUNK)
    valid = (key_chunk >= 0)[None, :, None, None, None, :]
    scores = jnp.where(valid, scores, -jnp.inf)
    sink = sinks.astype(jnp.float32).reshape(1, 1, N_KV_HEADS, GROUP, 1, 1)
    m = jnp.maximum(jnp.max(scores, axis=-1, keepdims=True), sink)
    pr = jnp.exp(scores - m)
    denom = jnp.sum(pr, axis=-1, keepdims=True) + jnp.exp(sink - m)
    pr = (pr / denom).astype(v.dtype)
    out = jnp.einsum('bnhgqk,bnkhd->bnqhgd', pr, vb)
    return out.reshape(B, S, ATTN_DIM)

def _normal(k, shape, scale):
    return jax.random.normal(k, shape, jnp.float32) * scale

def setup_inputs(seed: int = 0) -> dict:
    key = jax.random.key(seed)
    ks = jax.random.split(key, 24)
    L, D = DEPTH, D_MODEL
    gain = lambda k, n: 1.0 + _normal(k, (L, n), 0.05)
    return {
        "x": _normal(ks[0], (BATCH, SEQ, D), 1.0),
        "p": _normal(ks[1], (DEPTH, BATCH, SEQ, PLE_DIM), 1.0),
        "positions": (jnp.arange(SEQ, dtype=jnp.int32)[None, :]
                      + jax.random.randint(ks[2], (BATCH, 1), 0, 1024, dtype=jnp.int32)),
        "g_pre_mix": gain(ks[3], D),
        "w_in": _normal(ks[4], (L, D, IN_DIM), D ** -0.5),
        "conv_dw_w": _normal(ks[5], (L, CONV_WIDTH, CONV_DIM), CONV_WIDTH ** -0.5),
        "conv_dw_b": _normal(ks[6], (L, CONV_DIM), 0.02),
        "conv_ln_g": gain(ks[7], CONV_DIM),
        "conv_ln_b": _normal(ks[8], (L, CONV_DIM), 0.02),
        "w_conv_out": _normal(ks[9], (L, CONV_DIM, D), CONV_DIM ** -0.5),
        "attn_sinks": _normal(ks[10], (L, N_HEADS), 1.0),
        "w_attn_out": _normal(ks[11], (L, ATTN_DIM, D), ATTN_DIM ** -0.5),
        "w_out": _normal(ks[12], (L, D, D), D ** -0.5),
        "g_post_mix": gain(ks[13], D),
        "g_pre_ffn": gain(ks[14], D),
        "w_up": _normal(ks[15], (L, D, 2 * D_FF), D ** -0.5),
        "ffn_dw_w": _normal(ks[16], (L, FFN_CONV_WIDTH, D_FF), FFN_CONV_WIDTH ** -0.5),
        "ffn_dw_b": _normal(ks[17], (L, D_FF), 0.02),
        "w_down": _normal(ks[18], (L, D_FF, D), D_FF ** -0.5),
        "g_post_ffn": gain(ks[19], D),
        "w_ple": _normal(ks[20], (L, PLE_DIM, D), PLE_DIM ** -0.5),
        "w_ple_gate": _normal(ks[21], (L, D, D), D ** -0.5),
    }

def reference(x, p, positions, g_pre_mix, w_in, conv_dw_w, conv_dw_b, conv_ln_g, conv_ln_b,
              w_conv_out, attn_sinks, w_attn_out, w_out, g_post_mix, g_pre_ffn, w_up,
              ffn_dw_w, ffn_dw_b, w_down, g_post_ffn, w_ple, w_ple_gate):
    B, S, D = x.shape
    h = x
    split_at = [2 * CONV_DIM, 2 * CONV_DIM + ATTN_DIM, 2 * CONV_DIM + ATTN_DIM + KV_DIM,
                2 * CONV_DIM + ATTN_DIM + 2 * KV_DIM]
    for i in range(DEPTH):
        u = rms_norm(h, g_pre_mix[i])
        z = u @ w_in[i]
        z_glu, q, k, v, z_gate = jnp.split(z, split_at, axis=-1)

        a, b = jnp.split(z_glu, 2, axis=-1)
        c = a * jax.nn.sigmoid(b)
        c = causal_depthwise_conv(c, conv_dw_w[i], conv_dw_b[i])
        c = jax.nn.silu(layer_norm(c, conv_ln_g[i], conv_ln_b[i]))
        y_conv = c @ w_conv_out[i]

        q = apply_rope(q.reshape(B, S, N_HEADS, HEAD_DIM), positions)
        k = apply_rope(k.reshape(B, S, N_KV_HEADS, HEAD_DIM), positions)
        v = v.reshape(B, S, N_KV_HEADS, HEAD_DIM)
        y_attn = sliding_window_sink_attention(q, k, v, attn_sinks[i]) @ w_attn_out[i]

        gates = jax.nn.sigmoid(z_gate).reshape(B, S, N_BRANCHES, D)
        y = gates[:, :, 0, :] * y_conv + gates[:, :, 1, :] * y_attn
        h = h + rms_norm(y @ w_out[i], g_post_mix[i])

        u = rms_norm(h, g_pre_ffn[i])
        gate, val = jnp.split(u @ w_up[i], 2, axis=-1)
        gate = causal_depthwise_conv(gate, ffn_dw_w[i], ffn_dw_b[i])
        f = (jax.nn.gelu(gate, approximate=True) * val) @ w_down[i]
        h = h + rms_norm(f, g_post_ffn[i])

        h = h + (p[i] @ w_ple[i]) * jax.nn.sigmoid(h @ w_ple_gate[i])
    return h


_drawn_inputs = setup_inputs


def setup_inputs(seed=0):
    import zlib

    import numpy as np

    out = dict(_drawn_inputs(seed))
    spreads = {}
    factors = {'conv_ln_b': 3.695, 'attn_sinks': 8.0, 'ffn_dw_b': 5.066}
    for name, (base, spread) in spreads.items():
        noise = np.random.default_rng([zlib.crc32(name.encode()), seed]).standard_normal(out[name].shape)
        drawn = base * np.exp(spread * noise) if base else spread * noise
        out[name] = __import__('jax').numpy.asarray(drawn.astype(out[name].dtype))
    for name, factor in factors.items():
        out[name] = (out[name] * factor).astype(out[name].dtype)
    return out
```

```python
from contextlib import ExitStack

import numpy as np

import concourse.bass as bass
from concourse import mybir

F32 = mybir.dt.float32
F32R = mybir.dt.float32r
I32 = mybir.dt.int32
ALU = mybir.AluOpType
ACT = mybir.ActivationFunctionType
AX = mybir.AxisListType
ds = bass.ds

P = 128
D = 1024
SEQ = 2048
T = 512
CHUNKS = SEQ // T
TT = T // P
KD_ = D // P
CONV = 512
NC = CONV // P
TAPS = 31
HALO = TAPS - 1
EARLY = 15
LATE = TAPS - EARLY
HEADS = 8
HD = 64
PAIRS = HEADS // 2
CH = 64
SUB = T // CH
FF = 2816
NF = FF // P
F1 = 16
F2 = NF - F1
PLE = 256
NP = PLE // P
EPS = 1e-6
SCALE = HD ** -0.5

SLOTS = 2
B_GLU = 0
B_QKV = B_GLU + 2 * NC
B_GA = B_QKV + PAIRS + 2
B_MRG = B_GA + KD_
B_WO = B_MRG + 2 * KD_
B_UP1 = B_WO + KD_
B_DN1 = B_UP1 + 2 * F1
B_UP2 = B_DN1 + 2 * KD_
B_DN2 = B_UP2 + 2 * F2
B_WP = B_DN2 + F2 * KD_ // 8
B_PG = B_WP + NP * KD_ // 8
NB = B_PG + KD_
assert NB == 122 and all(b % 2 == 0 for b in (B_QKV, B_GA, B_MRG, B_WO, B_UP1, B_DN1, B_UP2, B_DN2, B_WP, B_PG, NB))

COLS = {}


def _col(name, n):
    COLS[name] = sum(w for _, w in COLS.values()), n


for _name, _n in (("g_pre_mix", KD_), ("conv_w", NC * TAPS), ("conv_b", NC), ("ln_g", NC), ("ln_b", NC),
                  ("g_post_mix", KD_), ("g_pre_ffn", KD_), ("ffn_w", NF * 3), ("ffn_b", NF), ("g_post_ffn", KD_),
                  ("sinks", PAIRS), ("inv_freq", 1), ("sin_sign", 1), ("eps", 1)):
    _col(_name, _n)
NCOL = sum(w for _, w in COLS.values())

N_X, N_LN, N_POST, N_PRE, N_PF = range(5)
NORMS = 5
Q_LN, Q_POST, Q_PRE, Q_PF = 0, NC, NC + KD_, NC + 2 * KD_
NQ = NC + 3 * KD_

TWO_PI = 2 * np.pi
C1 = 6.28125
C2 = float(np.floor((TWO_PI - C1) * 2 ** 20) / 2 ** 20)
C3 = float(np.float32(TWO_PI - C1 - C2))
MAGIC = 1.5 * 2 ** 23
PI_IN = 3.1415925


def build_kernel(nc, x, p, positions, weights, columns, identity, out):
    with ExitStack() as ctx:
        top = [(nc.sbuf_base + 63) // 64 * 64]

        def region(nbytes):
            at = top[0]
            top[0] += (nbytes + 63) // 64 * 64
            assert top[0] <= nc.sbuf_usable_end, top[0]
            return at

        def sb(name, shape, dt, at=None):
            n = 4 * int(np.prod(shape[1:]))
            return nc.alloc_sbuf_tensor_at(name, shape, dt, offset=region(n) if at is None else at)

        K = 1024
        w_stage = sb("w_stage", [P, SLOTS, 8, P], F32)
        w_hi = sb("w_hi", [P, SLOTS, 8, P], F32R)
        w_lo = sb("w_lo", [P, SLOTS, 8, P], F32R)
        at = region(64 * K)
        u_hi = sb("u_hi", [P, KD_, T], F32R, at)
        u_lo = sb("u_lo", [P, KD_, T], F32R, at + 16 * K)
        ca_hi = sb("ca_hi", [P, KD_, T], F32R, at + 32 * K)
        ca_lo = sb("ca_lo", [P, KD_, T], F32R, at + 48 * K)
        f_hi = sb("f_hi", [P, F1, T], F32R, at)
        f_lo = sb("f_lo", [P, F1, T], F32R, at + 32 * K)
        y_hi = sb("y_hi", [P, KD_, T], F32R)
        y_lo = sb("y_lo", [P, KD_, T], F32R)
        h = sb("h", [P, KD_, T], F32)
        at = region(16 * K)
        x_rows = sb("x_rows", [P, TT, D], F32, at)
        gate_a = sb("gate_a", [P, KD_, T], F32, at)
        acc = sb("acc", [P, KD_, T], F32, at)
        at = region(4 * (NC * (HALO + T) + NC * T))
        conv_in = sb("conv_in", [P, NC, HALO + T], F32, at)
        conv_acc = sb("conv_acc", [P, NC, T], F32, at + 4 * NC * (HALO + T))
        p_rows = sb("p_rows", [P, TT, PLE], F32, at)
        ple = sb("ple", [P, KD_, T], F32, at)
        conv_halo = sb("conv_halo", [P, NC, HALO], F32)
        ffn_halo = sb("ffn_halo", [P, NF, 2], F32)
        k_dup = sb("k_dup", [P, 2, CH + T], F32)
        v_odd = sb("v_odd", [P, TT, P], F32)
        v_even = sb("v_even", [P, TT + 1, P], F32)
        at = region(22 * K)
        junk = sb("junk", [P, D], F32, at)
        u_tmp = sb("u_tmp", [P, 2, T], F32, at + 4 * K)
        qT = sb("qT", [P, PAIRS, T], F32, at)
        cos_t = sb("cos_t", [P, T], F32, at + 8 * K)
        sin_t = sb("sin_t", [P, T], F32, at + 10 * K)
        pos_i = sb("pos_i", [P, T], I32, at + 12 * K)
        angle = sb("angle", [P, T], F32, at + 14 * K)
        turns = sb("turns", [P, T], F32, at + 16 * K)
        trig = sb("trig", [P, 2, T], F32, at + 18 * K)
        glu_sg = sb("glu_sg", [P, 2, T], F32, at + 12 * K)
        rope_a = sb("rope_a", [P, 2, T], F32, at + 12 * K)
        rope_b = sb("rope_b", [P, 2, T], F32, at + 16 * K)
        prob = sb("prob", [P, 2, PAIRS, P], F32, at + 8 * K)
        probT = sb("probT", [P, 2, PAIRS, P], F32, at + 12 * K)
        v_cur = sb("v_cur", [P, 2, 2, 2, HD], F32, at + 16 * K)
        q_diag = sb("q_diag", [P, 2, PAIRS, P], F32, at + 18 * K)
        silu_c = sb("silu_c", [P, 2, T], F32, at + 8 * K)
        gate_b = sb("gate_b", [P, 2, T], F32, at)
        part_a = sb("part_a", [P, 2, T], F32, at + 4 * K)
        part_b = sb("part_b", [P, 2, T], F32, at + 8 * K)
        y_tmp = sb("y_tmp", [P, 2, T], F32, at + 12 * K)
        h_tmp = sb("h_tmp", [P, 2, T], F32, at + 12 * K)
        g_in = sb("g_in", [P, 2, 2 + T], F32, at)
        g_conv = sb("g_conv", [P, 2, T], F32, at + 4 * K + 64)
        g_act = sb("g_act", [P, 2, T], F32, at + 8 * K + 64)
        f_val = sb("f_val", [P, 2, T], F32, at + 12 * K + 64)
        f_tmp = sb("f_tmp", [P, 2, T], F32, at + 16 * K + 64)
        ple_sg = sb("ple_sg", [P, 2, T], F32, at)
        ple_t = sb("ple_t", [P, 2, T], F32, at + 4 * K)
        ssum = sb("ssum", [P, T], F32)
        sq = sb("sq", [P, 2, T], F32)
        diag = sb("diag", [P, TT, P], F32)
        r_ffn = sb("r_ffn", [P, T], F32)
        ident = sb("ident", [P, P], F32)
        ones = sb("ones", [P, P], F32)
        col = sb("col", [P, NCOL], F32)
        prev_bias = sb("prev_bias", [P, CH], F32)
        x_ss = sb("x_ss", [P, TT], F32)
        n_root = sb("n_root", [P, TT], F32)
        n_var = sb("n_var", [P, TT], F32)
        n_r = sb("n_r", [P, TT], F32)
        n_t = sb("n_t", [P, TT], F32)
        s_max = sb("s_max", [P, 2, PAIRS], F32)
        s_m = sb("s_m", [P, 2, PAIRS], F32)
        s_neg = sb("s_neg", [P, 2, PAIRS], F32)
        s_sink = sb("s_sink", [P, 2, PAIRS], F32)
        s_sinke = sb("s_sinke", [P, 2, PAIRS], F32)
        s_den = sb("s_den", [P, 2, PAIRS], F32)
        s_rec = sb("s_rec", [P, 2, PAIRS], F32)

        ps = ctx.enter_context(nc.psum_tensor("ps", [P, 8, T], F32))
        ATT = 4
        PV = 6
        SMALL, BC = 6, 7
        QK_BANK = 2, 3, 0, 1, 4
        V_BANK = 5
        GA_BANK = 2
        PG_BANK = 2, 3, 4, 5, 0, 1, 2, 3
        OT_BANK = 6, 7, 4, 5

        def column(name, i=0):
            first, n = COLS[name]
            return col[:, ds(first + i, 1)] if not isinstance(i, int) else col[:, first + i:first + i + 1]

        def column_range(name):
            first, n = COLS[name]
            return col[:, first:first + n]

        def four(ap):
            return ap.rearrange("p (t n) -> p t n", t=TT)

        def sem(name):
            return ctx.enter_context(nc.semaphore(name))

        const_loaded, x_loaded, pos_loaded, p_loaded, out_stored = map(
            sem, ("const_loaded", "x_loaded", "pos_loaded", "p_loaded", "out_stored"))
        w_loaded = [sem("w_loaded_even"), sem("w_loaded_odd")]
        setup = sem("setup")
        block_done = sem("block_done")
        w_hi_ready = sem("w_hi_ready")
        w_lo_ready = sem("w_lo_ready")
        x_squared = sem("x_squared")
        xt_done, h_loaded, ut_ready, u_hi_ready, u_ready = map(
            sem, ("xt_done", "h_loaded", "ut_ready", "u_hi_ready", "u_ready"))
        root_ready, norm_step, diag_ready, bc_ready = map(sem, ("root_ready", "norm_step", "diag_ready", "bc_ready"))
        sq_ready, ss_added, ss_zeroed, ssum_done = map(sem, ("sq_ready", "ss_added", "ss_zeroed", "ssum_done"))
        trig_step, trig_ready, trig_done = map(sem, ("trig_step", "trig_ready", "trig_done"))
        glu_sig, glu_done, halo_in, conv_tap = map(sem, ("glu_sig", "glu_done", "halo_in", "conv_tap"))
        rope_swapped, rope_step, rope_done, k_halo, v_step, v_ready = map(
            sem, ("rope_swapped", "rope_step", "rope_done", "k_halo", "v_step", "v_ready"))
        q_diag_ready, q_zeroed, v_cur_ready, qk_done, sm_step, sm_ready, exp_done, pn_ready, t_done, pt_ready, pv_done, \
            ao_hi, ao_lo, gate_a_ready = map(sem, (
                "q_diag_ready", "q_zeroed", "v_cur_ready", "qk_done", "sm_step", "sm_ready", "exp_done", "pn_ready", "t_done",
                "pt_ready", "pv_done", "ao_hi", "ao_lo", "gate_a_ready"))
        ln_summed, mean_ready, ln_centred, ln_scaled, silu_ready, c_hi, c_lo = map(
            sem, ("ln_summed", "mean_ready", "ln_centred", "ln_scaled", "silu_ready", "c_hi", "c_lo"))
        gate_b_ready, part_a_ready, merged, yt_ready, y_hi_ready, y_lo_ready, y2_out = map(
            sem, ("gate_b_ready", "part_a_ready", "merged", "yt_ready", "y_hi_ready", "y_lo_ready", "y2_out"))
        mid_step, h_mid, u2_hi, u2_lo, r_ffn_ready = map(sem, ("mid_step", "h_mid", "u2_hi", "u2_lo", "r_ffn_ready"))
        ffn_step, g_in_ready, tap0_ready, conv3_done, gelu_ready, val_read, ft_ready, f_hi_ready, f_lo_ready = map(
            sem, ("ffn_step", "g_in_ready", "tap0_ready", "conv3_done", "gelu_ready", "val_read", "ft_ready",
                  "f_hi_ready", "f_lo_ready"))
        d1_out, d2_acc, pt_done, p_hi, p_lo, ple_out = map(sem, ("d1_out", "d2_acc", "pt_done", "p_hi", "p_lo", "ple_out"))
        h3_step, h3_mid, h3_hi, h3_lo, ple_sig, ple_mul, out_ready, ot_done, os_out = map(
            sem, ("h3_step", "h3_mid", "h3_hi", "h3_lo", "ple_sig", "ple_mul", "out_ready", "ot_done", "os_out"))
        SETUPS = 7

        block = ctx.enter_context(nc.Block())

        @block.sync
        def _(sp):
            sp.dma_start(col[:, :], columns).then_inc(const_loaded, 16)
            sp.dma_start(ident[:, :], identity).then_inc(const_loaded, 16)
            with sp.Fori(0, CHUNKS) as c:
                def load_blocks(first, count):
                    with sp.Fori(0, count // 2) as i:
                        for par in range(2):
                            sp.wait_ge(w_lo_ready, c * NB + 2 * i + (first + par + 1))
                            sp.dma_start(w_stage[:, par].rearrange("p k n -> p (k n)"),
                                         weights[2 * i + (first + par)]).then_inc(w_loaded[par], 16)

                sp.wait_ge(h3_lo, c * KD_ + 1)
                sp.dma_start(x_rows[:, :, :], x[ds(c * T, T), :].rearrange("(t p) d -> p t d", p=P)).then_inc(x_loaded, 16)
                sp.dma_start(pos_i[:, :], positions[0:1, ds(c * T, T)].broadcast_to([P, T])).then_inc(pos_loaded, 16)
                load_blocks(0, B_UP1)
                sp.wait_ge(c_lo, c * NC + NC)
                sp.dma_start(p_rows[:, :, :], p[ds(c * T, T), :].rearrange("(t p) d -> p t d", p=P)).then_inc(p_loaded, 16)
                load_blocks(B_UP1, NB - B_UP1)

        @block.gpsimd
        def _(pool):
            pool.sem_inc(w_lo_ready, SLOTS)
            with pool.Fori(0, CHUNKS * NB // 2) as i:
                for par in range(2):
                    pool.wait_ge(w_hi_ready, 2 * i + (par + 1))
                    nc.gpsimd.tensor_tensor(w_lo[:, par], w_stage[:, par], w_hi[:, par].bitcast(F32),
                                            ALU.subtract).then_inc(w_lo_ready, 1)

        @block.scalar
        def _(act):
            copy = nc.scalar.activation
            act.sem_inc(out_stored, 16 * KD_)
            act.sem_inc(gate_a_ready, 2)
            act.sem_inc(y2_out, 4)
            act.sem_inc(d1_out, 2)
            act.sem_inc(ple_sig, 2)
            act.sem_inc(os_out, 4)
            act.wait_ge(const_loaded, 32)
            act.wait_ge(setup, SETUPS)
            with act.Fori(0, CHUNKS) as c:
                def split(half, par):
                    act.wait_ge(block_done, c * NB + 2 * half + (par + 1))
                    act.wait_ge(w_loaded[par], (c * (NB // 2) + half + 1) * 16)
                    copy(w_hi[:, par], w_stage[:, par], ACT.Copy).then_inc(w_hi_ready, 1)

                def done(b):
                    act.wait_ge(block_done, c * NB + b + (1 + SLOTS))

                def square(q, src, slot):
                    act.wait_ge(ss_added, c * NQ + q + 1)
                    copy(sq[:, slot], src, ACT.Square).then_inc(sq_ready, 1)

                def root(n, src, count):
                    copy(n_root[:, :], src, ACT.Sqrt, bias=column("eps"), scale=1.0 / count).then_inc(root_ready, 1)

                split(0, 0)
                split(0, 1)
                act.wait_ge(x_loaded, c * 16 + 16)
                for t in range(TT):
                    copy(junk[:, :], x_rows[:, t], ACT.Square, accum_out=x_ss[:, t:t + 1]).then_inc(x_squared, 1)
                    act.wait_ge(x_squared, c * TT + t + 1)
                root(N_X, x_ss[:, :], D)
                with act.Fori(0, 2) as i:
                    for n in range(4):
                        act.wait_ge(xt_done, c * KD_ + 4 * i + (n + 1))
                        copy(h[:, 4 * i + n], ps[:, n], ACT.Copy).then_inc(h_loaded, 1)
                def u_tiles(i):
                    for n in range(2):
                        act.wait_ge(ut_ready, c * KD_ + 2 * i + (n + 1))
                        copy(u_hi[:, 2 * i + n], u_tmp[:, n], ACT.Copy).then_inc(u_hi_ready, 1)

                with act.Fori(0, 2) as i:
                    u_tiles(i)
                split(B_GLU // 2 + 1, 0)
                u_tiles(2)
                split(B_GLU // 2 + 1, 1)
                u_tiles(3)
                act.wait_ge(trig_ready, c * 2 + 1)
                copy(sin_t[:, :], trig[:, 0], ACT.Sin, scale=column("sin_sign")).then_inc(trig_done, 1)
                act.wait_ge(trig_ready, c * 2 + 2)
                copy(cos_t[:, :], trig[:, 1], ACT.Sin).then_inc(trig_done, 1)
                act.wait_ge(out_stored, c * (16 * KD_) + 16 * KD_)
                split(B_GLU // 2 + 2, 0)
                split(B_GLU // 2 + 2, 1)
                for j in range(NC):
                    if j >= 2:
                        split(B_GLU // 2 + j + 1, 0)
                    done(B_GLU + max(2 * j + 1, 3))
                    act.wait_ge(glu_done, c * NC + j + 1)
                    copy(glu_sg[:, j % 2], ps[:, 2 * j + 1], ACT.Sigmoid).then_inc(glu_sig, 1)
                    if j >= 2:
                        split(B_GLU // 2 + j + 1, 1)
                for j in range(PAIRS + 1):
                    split(B_QKV // 2 + (j + 2) // 2, j % 2)
                    done(B_QKV + j)
                    if j == 0:
                        act.wait_ge(glu_done, c * NC + NC + 2)
                    if j >= 2:
                        act.wait_ge(rope_done, c * (PAIRS + 1) + j - 1)
                    for q in range(4):
                        last = copy(rope_b[32 * q:32 * q + 32, j % 2], ps[32 * (q ^ 1):32 * (q ^ 1) + 32, QK_BANK[j]],
                                    ACT.Copy)
                    last.then_inc(rope_swapped, 1)
                split(B_QKV // 2 + 3, 1)
                done(B_QKV + PAIRS + 1)
                v_new = four(ps[:, V_BANK])
                copy(v_even[CH:P, 0], v_even[CH:P, TT], ACT.Copy)
                copy(v_odd[:, :, :], v_new, ACT.Copy).then_inc(v_step, 1)
                act.wait_ge(v_step, c + 1)
                copy(v_even[0:CH, 0:TT], v_new[0:CH], ACT.Copy)
                copy(v_even[CH:P, 1:TT + 1], v_new[CH:P], ACT.Copy).then_inc(v_ready, 1)
                act.wait_ge(rope_done, (c + 1) * (PAIRS + 1))
                act.wait_ge(q_zeroed, c + 1)
                act.wait_ge(v_ready, c + 1)

                def attend_q(i):
                    for s in range(2):
                        now = ds(2 * CH * i + CH * s, CH)
                        copy(q_diag[0:CH, s, :, 0:CH], qT[0:CH, :, now], ACT.Copy)
                        copy(q_diag[CH:P, s, :, CH:P], qT[CH:P, :, now], ACT.Copy).then_inc(q_diag_ready, 1)

                def attend(i, more):
                    for s, v in enumerate((v_even, v_odd)):
                        src = v[:, ds(i, 1)].rearrange("p o (g d) -> p (o g) d", g=2)
                        for twice in range(2):
                            last = copy(v_cur[:, s, :, twice], src, ACT.Copy)
                        last.then_inc(v_cur_ready, 1)
                    for s in range(2):
                        act.wait_ge(sm_ready, c * SUB + 2 * i + (s + 1))
                        for a in range(PAIRS):
                            copy(prob[:, s, a], ps[:, ATT + s, P * a:P * a + P], ACT.Exp, bias=s_neg[:, s, a:a + 1],
                                 scale=SCALE, accum_out=s_den[:, s, a:a + 1])
                        copy(s_sinke[:, s], s_sink[:, s], ACT.Exp).then_inc(exp_done, 1)
                    if more:
                        attend_q(i + 1)
                    split(B_GA // 2 + i + 1, 0)
                    split(B_GA // 2 + i + 1, 1)
                    for s in range(2):
                        act.wait_ge(t_done, c * SUB + 2 * i + (s + 1))
                        copy(probT[:, s], four(ps[:, PV + s]), ACT.Copy).then_inc(pt_ready, 1)
                    for s in range(2):
                        copy(gate_a[:, 2 * i + s], ps[:, GA_BANK + s], ACT.Sigmoid).then_inc(gate_a_ready, 1)
                    for s in range(2):
                        act.wait_ge(pv_done, c * SUB + 2 * i + (s + 1))
                        now = ds(2 * CH * i + CH * s, CH)
                        ao = four(ps[:, PV + s])
                        copy(ca_hi[0:CH, NC:, now], ao[0:CH, :, 0:CH], ACT.Copy)
                        copy(ca_hi[CH:P, NC:, now], ao[CH:P, :, CH:P], ACT.Copy).then_inc(ao_hi, 1)

                attend_q(0)
                with act.Fori(0, SUB // 2 - 1) as i:
                    attend(i, True)
                attend(SUB // 2 - 1, False)
                def gate_b_tile(i, n):
                    act.wait_ge(merged, c * KD_ + 2 * i + (n + 1))
                    copy(gate_b[:, n], ps[:, 2 * n], ACT.Sigmoid).then_inc(gate_b_ready, 1)

                def centred_square(j):
                    act.wait_ge(ln_centred, c * NC + j + 1)
                    square(Q_LN + j, conv_acc[:, j], j % 2)

                split(B_MRG // 2 + 1, 0)
                gate_b_tile(0, 0)
                centred_square(0)
                centred_square(1)
                split(B_MRG // 2 + 1, 1)
                centred_square(2)
                centred_square(3)
                gate_b_tile(0, 1)
                act.wait_ge(ssum_done, c * (NORMS - 1) + 1)
                root(N_LN, ps[:, SMALL, 0:TT], CONV)
                for j in range(NC):
                    act.wait_ge(ln_scaled, c * NC + j + 1)
                    if j >= 2:
                        act.wait_ge(c_lo, c * NC + j - 1)
                    copy(silu_c[:, j % 2], conv_acc[:, j], ACT.Silu, bias=column("ln_b", j)).then_inc(silu_ready, 1)
                    act.wait_ge(silu_ready, c * NC + j + 1)
                    copy(ca_hi[:, j], silu_c[:, j % 2], ACT.Copy).then_inc(c_hi, 1)
                def merge_y(i):
                    for n in range(2):
                        split(B_MRG // 2 + 2 * i + 2, n)
                        act.wait_ge(yt_ready, c * KD_ + 2 * i + (n + 1))
                        copy(y_hi[:, 2 * i + n], y_tmp[:, n], ACT.Copy).then_inc(y_hi_ready, 1)

                merge_y(0)
                with act.Fori(1, KD_ // 2) as i:
                    for n in range(2):
                        split(B_MRG // 2 + 2 * i + 1, n)
                        gate_b_tile(i, n)
                    merge_y(i)
                act.wait_ge(merged, c * KD_ + (KD_ + 2))
                with act.Fori(0, KD_ // 4) as i:
                    for n in range(4):
                        split(B_WO // 2 + 2 * i + (n // 2 + 1), n % 2)
                        square(Q_POST + 4 * i + n, ps[:, n], n % 2)
                        copy(acc[:, 4 * i + n], ps[:, n], ACT.Copy).then_inc(y2_out, 1)
                act.wait_ge(ssum_done, c * (NORMS - 1) + 2)
                root(N_POST, ps[:, SMALL, 0:TT], D)
                def mid_tiles(i):
                    for n in range(2):
                        act.wait_ge(ss_added, c * NQ + Q_PRE + 2 * i + (n + 1))
                        act.wait_ge(h_mid, c * KD_ + 2 * i + (n + 1))
                        copy(y_hi[:, 2 * i + n], h[:, 2 * i + n], ACT.Identity, bias=0.0,
                             scale=column("g_pre_ffn", 2 * i + n)).then_inc(u2_hi, 1)
                        copy(sq[:, n], h[:, 2 * i + n], ACT.Square).then_inc(sq_ready, 1)

                with act.Fori(0, 2) as i:
                    mid_tiles(i)
                split(B_UP1 // 2 + 1, 0)
                mid_tiles(2)
                split(B_UP1 // 2 + 1, 1)
                mid_tiles(3)
                split(B_UP1 // 2 + 2, 0)
                split(B_UP1 // 2 + 2, 1)
                act.wait_ge(ssum_done, c * (NORMS - 1) + 3)
                root(N_PRE, ps[:, SMALL, 0:TT], D)
                act.wait_ge(bc_ready, c * NORMS + N_PRE + 1)
                copy(r_ffn[:, :], ps[:, BC], ACT.Copy).then_inc(r_ffn_ready, 1)

                def up(i, n, first_block, first_tile, splits=True):
                    item = c * NF + 2 * i + (first_tile + n + 1)
                    if splits:
                        split(first_block // 2 + 2 * i + (n + 1), 0)
                    act.wait_ge(g_in_ready, item)
                    copy(g_conv[:, n], g_in[:, n, 0:T], ACT.Identity, bias=column("ffn_b", 2 * i + (first_tile + n)),
                         scale=column("ffn_w", 6 * i + 3 * (first_tile + n))).then_inc(tap0_ready, 1)
                    if splits:
                        split(first_block // 2 + 2 * i + (n + 1), 1)
                    act.wait_ge(conv3_done, item)
                    copy(g_act[:, n], g_conv[:, n], ACT.Gelu_apprx_tanh).then_inc(gelu_ready, 1)
                    act.wait_ge(ft_ready, item)
                    copy(f_hi[:, 2 * i + (first_tile % F1 + n)], f_tmp[:, n], ACT.Copy).then_inc(f_hi_ready, 1)

                up(0, 0, B_UP1, 0, splits=False)
                split(B_UP1 // 2 + 3, 0)
                up(0, 1, B_UP1, 0, splits=False)
                split(B_UP1 // 2 + 3, 1)
                up(1, 0, B_UP1, 0, splits=False)
                up(1, 1, B_UP1, 0)
                with act.Fori(2, F1 // 2) as i:
                    for n in range(2):
                        up(i, n, B_UP1, 0)
                with act.Fori(0, KD_ // 2) as i:
                    for n in range(2):
                        split(B_DN1 // 2 + 2 * i + (n + 1), 0)
                        split(B_DN1 // 2 + 2 * i + (n + 1), 1)
                        copy(acc[:, 2 * i + n], ps[:, n], ACT.Copy).then_inc(d1_out, 1)
                for k in range(NP):
                    act.wait_ge(pt_done, c * NP + k + 1)
                    copy(f_hi[:, F1 - NP + k], ps[:, ATT + k], ACT.Copy).then_inc(p_hi, 1)
                with act.Fori(0, F2 // 2) as i:
                    for n in range(2):
                        up(i, n, B_UP2, F1)
                nxt = B_DN2
                for j in range(KD_):
                    while nxt <= B_DN2 + (F2 * (j + 1) - 1) // 8:
                        split(nxt // 2 + 1, nxt % 2)
                        nxt += 1
                    act.wait_ge(d2_acc, c * KD_ + j + 1)
                    square(Q_PF + j, acc[:, j], j % 2)
                act.wait_ge(ssum_done, c * (NORMS - 1) + 4)
                root(N_PF, ps[:, SMALL, 0:TT], D)
                for j in range(6):
                    if j == 0:
                        split(B_WP // 2 + 1, 0)
                    done(B_WP + j // 4)
                    copy(ple[:, j], ps[:, j], ACT.Copy).then_inc(ple_out, 1)
                def h3_tiles(i):
                    for n in range(2):
                        act.wait_ge(h3_mid, c * KD_ + 2 * i + (n + 1))
                        copy(y_hi[:, 2 * i + n], h[:, 2 * i + n], ACT.Copy).then_inc(h3_hi, 1)

                split(B_PG // 2, 1)
                with act.Fori(0, 2) as i:
                    h3_tiles(i)
                split(B_PG // 2 + 1, 0)
                h3_tiles(2)
                split(B_PG // 2 + 1, 1)
                h3_tiles(3)
                for j in range(6, KD_):
                    copy(ple[:, j], ps[:, j - 6], ACT.Copy).then_inc(ple_out, 1)

                def ple_gate(j):
                    done(B_PG + max(j, 3))
                    act.wait_ge(out_ready, c * KD_ + j + 1)
                    copy(ple_sg[:, j % 2], ps[:, PG_BANK[j]], ACT.Sigmoid).then_inc(ple_sig, 1)

                def out_rows(f):
                    act.wait_ge(ot_done, c * KD_ + f + 1)
                    copy(ple[:, f], ps[:, OT_BANK[f % 4]], ACT.Copy).then_inc(os_out, 1)
                    act.wait_ge(os_out, c * KD_ + f + 5)
                    act.dma_start(out[ds(c * T, T), P * f:P * f + P].rearrange("(t p) d -> p t d", p=P),
                                  four(ple[:, f])).then_inc(out_stored, 16)

                split(B_PG // 2 + 2, 0)
                split(B_PG // 2 + 2, 1)
                ple_gate(0)
                ple_gate(1)
                split(B_PG // 2 + 3, 0)
                ple_gate(2)
                ple_gate(3)
                split(B_PG // 2 + 3, 1)
                ple_gate(4)
                out_rows(0)
                ple_gate(5)
                out_rows(1)
                ple_gate(6)
                out_rows(2)
                out_rows(3)
                ple_gate(7)
                for f in range(4, KD_):
                    out_rows(f)
            act.wait_ge(out_stored, (CHUNKS + 1) * 16 * KD_)

        @block.tensor
        def _(pe):
            pe.sem_inc(block_done, SLOTS)
            pe.wait_ge(const_loaded, 32)
            pe.wait_ge(setup, SETUPS)
            with pe.Fori(0, CHUNKS) as c:
                def ready(b):
                    pe.wait_ge(w_lo_ready, c * NB + b + (1 + SLOTS))

                def product(bank, par, kk, hi, lo, start, stop):
                    nc.tensor.matmul(bank, w_hi[:, par, kk], hi, start=start, stop=False)
                    nc.tensor.matmul(bank, w_hi[:, par, kk], lo, start=False, stop=False)
                    return nc.tensor.matmul(bank, w_lo[:, par, kk], hi, start=False, stop=stop)

                def full_block(b, par, bank, hi, lo, need=None):
                    ready(b)
                    for k in range(8):
                        if need is not None:
                            pe.wait_ge(need[0], need[1] + (k + 1))
                        last = product(ps[:, bank], par, k, hi[:, k], lo[:, k], k == 0, k == 7)
                    last.then_inc(block_done, 1)

                def four_by_tile(b, banks, hi, lo, need):
                    for k in range(8):
                        if k % 2 == 0:
                            ready(b + k // 2)
                        pe.wait_ge(need[0], need[1] + (k + 1))
                        for o in range(4):
                            last = product(ps[:, banks[o]], k // 2 % 2, k % 2 * 4 + o, hi[:, k], lo[:, k], k == 0, k == 7)
                        if k % 2 == 1:
                            last.then_inc(block_done, 1)

                def token_sums(n, q_end):
                    pe.wait_ge(ss_added, c * NQ + (q_end + 2))
                    for t in range(TT):
                        last = nc.tensor.matmul(ps[:, SMALL, t:t + 1], ssum[:, P * t:P * t + P], ones[:, 0:1],
                                                start=True, stop=True)
                    last.then_inc(ssum_done, 1)

                def spread(n):
                    pe.wait_ge(diag_ready, c * NORMS + (n + 1))
                    nc.tensor.matmul(ps[:, BC], ones[:, :], diag[:, :, :].rearrange("p t n -> p (t n)"),
                                     start=True, stop=True).then_inc(bc_ready, 1)

                pe.wait_ge(x_loaded, c * 16 + 16)
                pe.wait_ge(ple_sig, c * KD_ + 2)
                for f in range(KD_):
                    if f >= 4:
                        pe.wait_ge(h_loaded, c * KD_ + f - 3)
                    for t in range(TT):
                        last = nc.tensor.transpose(ps[:, f % 4, P * t:P * t + P], x_rows[:, t, P * f:P * f + P], ident[:, :])
                    last.then_inc(xt_done, 1)
                pe.wait_ge(os_out, c * KD_ + 4)
                spread(N_X)
                pe.wait_ge(h_loaded, c * KD_ + KD_)
                four_by_tile(B_GLU, (0, 1, 2, 3), u_hi, u_lo, (u_ready, c * KD_))
                for b in range(4, 8):
                    full_block(B_GLU + b, b % 2, b, u_hi, u_lo)
                for j in range(PAIRS + 1):
                    glu_tile = QK_BANK[j] // 2
                    pe.wait_ge(glu_done, c * NC + (glu_tile + 3))
                    full_block(B_QKV + j, j % 2, QK_BANK[j], u_hi, u_lo)
                ready(B_QKV + PAIRS + 1)
                for t in range(TT):
                    tok = slice(P * t, P * t + P)
                    for k in range(8):
                        nc.tensor.matmul(ps[:, V_BANK, tok], u_hi[:, k, tok], w_hi[:, 1, k], start=(k == 0), stop=False)
                        nc.tensor.matmul(ps[:, V_BANK, tok], u_lo[:, k, tok], w_hi[:, 1, k], start=False, stop=False)
                        last = nc.tensor.matmul(ps[:, V_BANK, tok], u_hi[:, k, tok], w_lo[:, 1, k], start=False, stop=(k == 7))
                last.then_inc(block_done, 1)
                def scores(i):
                    for s in range(2):
                        pe.wait_ge(q_diag_ready, c * SUB + 2 * i + (s + 1))
                        for a in range(PAIRS):
                            lhs = q_diag[:, s, a]
                            g = a // 2
                            if s == 0:
                                nc.tensor.matmul(ps[:, ATT, P * a:P * a + CH], lhs, k_dup[:, g, ds(2 * CH * i + CH, CH)],
                                                 start=True, stop=True)
                                last = nc.tensor.matmul(ps[:, ATT, P * a + CH:P * a + P], lhs, k_dup[:, g, ds(2 * CH * i, CH)],
                                                        start=True, stop=True)
                            else:
                                last = nc.tensor.matmul(ps[:, ATT + 1, P * a:P * a + P], lhs,
                                                        k_dup[:, g, ds(2 * CH * i + CH, 2 * CH)], start=True, stop=True)
                        last.then_inc(qk_done, 1)

                def attend(i, more):
                    for n in range(2):
                        ready(B_GA + 2 * i + n)
                        pe.wait_ge(gate_a_ready, c * KD_ + 2 * i + (n + 1))
                        for k in range(8):
                            last = product(ps[:, GA_BANK + n], n, k, u_hi[:, k], u_lo[:, k], k == 0, k == 7)
                        last.then_inc(block_done, 1)
                    for s in range(2):
                        pe.wait_ge(pn_ready, c * SUB + 2 * i + (s + 1))
                        pe.wait_ge(ao_lo, c * SUB + 2 * i + (s + 1))
                        for a in range(PAIRS):
                            last = nc.tensor.transpose(ps[:, PV + s, P * a:P * a + P], prob[:, s, a], ident[:, :])
                        last.then_inc(t_done, 1)
                    if more:
                        scores(i + 1)
                    for s in range(2):
                        pe.wait_ge(pt_ready, c * SUB + 2 * i + (s + 1))
                        pe.wait_ge(v_cur_ready, c * SUB + 2 * i + (s + 1))
                        for a in range(PAIRS):
                            last = nc.tensor.matmul(ps[:, PV + s, P * a:P * a + P],
                                                    v_cur[:, s, a // 2].rearrange("p t d -> p (t d)"), probT[:, s, a],
                                                    start=True, stop=True)
                        last.then_inc(pv_done, 1)

                pe.wait_ge(rope_done, (c + 1) * (PAIRS + 1))
                pe.wait_ge(v_ready, c + 1)
                scores(0)
                with pe.Fori(0, SUB // 2 - 1) as i:
                    attend(i, True)
                attend(SUB // 2 - 1, False)

                def gate_b_part(i, n, ks):
                    if 0 in ks:
                        pe.wait_ge(merged, c * KD_ + 2 * i + (n + 1))
                        ready(B_MRG + 4 * i + n)
                    for k in ks:
                        last = product(ps[:, 2 * n], n, k, u_hi[:, k], u_lo[:, k], k == 0, k == 7)
                    if 7 in ks:
                        last.then_inc(block_done, 1)

                def attention_out(i, n):
                    ready(B_MRG + 4 * i + 2 + n)
                    for k in range(NC, 8):
                        product(ps[:, ATT + n], n, k, ca_hi[:, k], ca_lo[:, k], k == NC, k == 7)

                def conv_out(n):
                    for k in range(NC):
                        pe.wait_ge(c_lo, c * NC + (k + 1))
                        last = product(ps[:, 2 * n + 1], n, k, ca_hi[:, k], ca_lo[:, k], k == 0, k == NC - 1)
                    last.then_inc(block_done, 1)

                gate_b_part(0, 0, range(0, 8))
                pe.wait_ge(gate_a_ready, c * KD_ + (KD_ + 2))
                gate_b_part(0, 1, range(0, 4))
                pe.wait_ge(ao_lo, c * SUB + (SUB + 2))
                pe.wait_ge(ln_summed, c * (NC - 1) + NC - 1)
                nc.tensor.matmul(ps[:, BC], ones[:, :], ssum[:, :], start=True, stop=True).then_inc(mean_ready, 1)
                gate_b_part(0, 1, range(4, 8))
                attention_out(0, 0)
                attention_out(0, 1)
                token_sums(N_LN, Q_LN + NC)
                spread(N_LN)
                conv_out(0)
                conv_out(1)
                with pe.Fori(1, KD_ // 2) as i:
                    gate_b_part(i, 0, range(8))
                    gate_b_part(i, 1, range(8))
                    for n in range(2):
                        attention_out(i, n)
                        conv_out(n)
                with pe.Fori(0, KD_ // 4) as i:
                    pe.wait_ge(merged, c * KD_ + (KD_ + 2))
                    for n in range(4):
                        pe.wait_ge(y2_out, c * KD_ + 4 * i + (n + 1))
                        full_block(B_WO + 4 * i + n, n % 2, n, y_hi, y_lo, (y_lo_ready, c * KD_))
                token_sums(N_POST, Q_POST + KD_)
                spread(N_POST)
                pe.wait_ge(y2_out, c * KD_ + (KD_ + 4))
                four_by_tile(B_UP1, (0, 1, 2, 3), y_hi, y_lo, (u2_lo, c * KD_))
                token_sums(N_PRE, Q_PRE + KD_)
                full_block(B_UP1 + 4, 0, 4, y_hi, y_lo)
                spread(N_PRE)
                full_block(B_UP1 + 5, 1, 5, y_hi, y_lo)

                def up_pair(i, n, first_block, first_tile):
                    pe.wait_ge(val_read, c * NF + 2 * i + (first_tile + n + 1))
                    for half in range(2):
                        full_block(first_block + 4 * i + 2 * n + half, half, 2 * n + half, y_hi, y_lo)

                up_pair(1, 1, B_UP1, 0)
                with pe.Fori(2, F1 // 2) as i:
                    for n in range(2):
                        up_pair(i, n, B_UP1, 0)
                with pe.Fori(0, KD_ // 2) as i:
                    pe.wait_ge(val_read, c * NF + (F1 + 2))
                    for n in range(2):
                        pe.wait_ge(d1_out, c * KD_ + 2 * i + (n + 1))
                        for k in range(F1):
                            if k % 8 == 0:
                                ready(B_DN1 + 4 * i + 2 * n + k // 8)
                            pe.wait_ge(f_lo_ready, c * NF + (k + 1))
                            last = product(ps[:, n], k // 8, k % 8, f_hi[:, k], f_lo[:, k], k == 0, k == F1 - 1)
                            if k % 8 == 7:
                                last.then_inc(block_done, 1)
                pe.wait_ge(p_loaded, c * 16 + 16)
                for k in range(NP):
                    for t in range(TT):
                        last = nc.tensor.transpose(ps[:, ATT + k, P * t:P * t + P], p_rows[:, t, P * k:P * k + P], ident[:, :])
                    last.then_inc(pt_done, 1)
                with pe.Fori(0, F2 // 2) as i:
                    pe.wait_ge(d1_out, c * KD_ + (KD_ + 2))
                    for n in range(2):
                        up_pair(i, n, B_UP2, F1)
                pe.wait_ge(val_read, c * NF + (NF + 2))
                for j in range(KD_):
                    if j >= 4:
                        pe.wait_ge(d2_acc, c * KD_ + j - 3)
                    for k in range(F2):
                        q = F2 * j + k
                        if q % 8 == 0:
                            ready(B_DN2 + q // 8)
                        if j == 0:
                            pe.wait_ge(f_lo_ready, c * NF + (F1 + k + 1))
                        last = product(ps[:, j % 4], q // 8 % 2, q % 8, f_hi[:, k], f_lo[:, k], k == 0, k == F2 - 1)
                        if q % 8 == 7:
                            last.then_inc(block_done, 1)

                def ple_out_tile(j):
                    if j == 0:
                        pe.wait_ge(p_lo, c * NP + NP)
                    if j < 4:
                        pe.wait_ge(d2_acc, c * KD_ + j + 5)
                    if j >= 6:
                        pe.wait_ge(ple_out, c * KD_ + j - 5)
                    for k in range(NP):
                        q = NP * j + k
                        if q % 8 == 0:
                            ready(B_WP + q // 8)
                        last = product(ps[:, j % 6], q // 8, q % 8, f_hi[:, F1 - NP + k], f_lo[:, F1 - NP + k], k == 0, k == NP - 1)
                        if q % 8 == 7:
                            last.then_inc(block_done, 1)

                for j in range(6):
                    if j == 3:
                        token_sums(N_PF, Q_PF + KD_)
                    ple_out_tile(j)
                spread(N_PF)
                ple_out_tile(6)
                ple_out_tile(7)
                def out_tile(f):
                    pe.wait_ge(out_ready, c * KD_ + f + 3)
                    if f >= 4:
                        pe.wait_ge(os_out, c * KD_ + f + 1)
                    for t in range(TT):
                        last = nc.tensor.transpose(ps[:, OT_BANK[f % 4], P * t:P * t + P], h[:, f, P * t:P * t + P],
                                                   ident[:, :])
                    last.then_inc(ot_done, 1)

                pe.wait_ge(ple_out, c * KD_ + 6)
                four_by_tile(B_PG, PG_BANK[0:4], y_hi, y_lo, (h3_lo, c * KD_ + 1))
                pe.wait_ge(ple_out, c * KD_ + KD_)
                full_block(B_PG + 4, 0, PG_BANK[4], y_hi, y_lo)
                full_block(B_PG + 5, 1, PG_BANK[5], y_hi, y_lo)
                out_tile(0)
                out_tile(1)
                pe.wait_ge(ple_sig, c * KD_ + (1 + 2))
                full_block(B_PG + 6, 0, PG_BANK[6], y_hi, y_lo)
                out_tile(2)
                out_tile(3)
                pe.wait_ge(ple_sig, c * KD_ + (2 + 2))
                full_block(B_PG + 7, 1, PG_BANK[7], y_hi, y_lo)
                for f in range(4, KD_):
                    out_tile(f)

        @block.vector
        def _(dve):
            V = nc.vector
            for s, n in ((glu_done, 2), (ao_lo, 2), (merged, 2), (val_read, 2), (ss_added, 2), (out_ready, 2), (h3_lo, 1)):
                dve.sem_inc(s, n)
            V.memset(ones[:, :], 1.0).then_inc(setup, 1)
            V.memset(prev_bias[:, :], -1e30).then_inc(setup, 1)
            V.memset(k_dup[:, :, :], 0.0).then_inc(setup, 1)
            V.memset(v_even[:, :, :], 0.0).then_inc(setup, 1)
            V.memset(conv_halo[:, :, :], 0.0).then_inc(setup, 1)
            V.memset(ffn_halo[:, :, :], 0.0).then_inc(setup, 1)
            V.memset(s_den[:, :, :], 0.0).then_inc(setup, 1)
            dve.wait_ge(const_loaded, 32)
            dve.wait_ge(setup, SETUPS)
            with dve.Fori(0, CHUNKS) as c:
                def done(b):
                    dve.wait_ge(block_done, c * NB + b + (1 + SLOTS))

                def norm(n, src, count):
                    at = (c * NORMS + n) * 6
                    dve.wait_ge(root_ready, c * NORMS + (n + 1))
                    V.tensor_scalar(n_var[:, :], src, 1.0 / count, EPS, ALU.mult, ALU.add).then_inc(norm_step, 1)
                    V.reciprocal(n_r[:, :], n_root[:, :]).then_inc(norm_step, 1)
                    dve.wait_ge(norm_step, at + 2)
                    V.tensor_tensor(n_t[:, :], n_r[:, :], n_r[:, :], ALU.mult).then_inc(norm_step, 1)
                    dve.wait_ge(norm_step, at + 3)
                    V.tensor_tensor(n_t[:, :], n_t[:, :], n_var[:, :], ALU.mult).then_inc(norm_step, 1)
                    dve.wait_ge(norm_step, at + 4)
                    V.tensor_scalar(n_t[:, :], n_t[:, :], -0.5, 1.5, ALU.mult, ALU.add).then_inc(norm_step, 1)
                    dve.wait_ge(norm_step, at + 5)
                    V.tensor_tensor(n_r[:, :], n_r[:, :], n_t[:, :], ALU.mult).then_inc(norm_step, 1)
                    dve.wait_ge(norm_step, at + 6)
                    V.tensor_tensor(diag[:, :, :], ident[:, :].unsqueeze(1).broadcast_to([P, TT, P]),
                                    n_r[:, :].unsqueeze(2).broadcast_to([P, TT, P]), ALU.mult).then_inc(diag_ready, 1)

                def zero_sum(which):
                    V.memset(ssum[:, :], 0.0).then_inc(ss_zeroed, 1)

                def add_square(q, slot, which):
                    dve.wait_ge(ss_zeroed, c * 4 + (which + 1))
                    dve.wait_ge(sq_ready, c * NQ + q + 1)
                    dve.wait_ge(ss_added, c * NQ + q + 2)
                    V.tensor_tensor(ssum[:, :], ssum[:, :], sq[:, slot], ALU.add).then_inc(ss_added, 1)

                dve.wait_ge(pos_loaded, c * 16 + 16)
                step = [0]

                def trig_link(ins):
                    step[0] += 1
                    ins.then_inc(trig_step, 1)
                    dve.wait_ge(trig_step, c * 14 + step[0])

                trig_link(V.tensor_copy(angle[:, :], pos_i[:, :]))
                trig_link(V.tensor_scalar(angle[:, :], angle[:, :], column("inv_freq"), None, ALU.mult))
                for s in range(2):
                    r = trig[:, s]
                    trig_link(V.tensor_scalar(turns[:, :], angle[:, :], float(1 / TWO_PI), 0.25 * s, ALU.mult, ALU.add))
                    trig_link(V.tensor_scalar(turns[:, :], turns[:, :], MAGIC, -MAGIC, ALU.add, ALU.add))
                    trig_link(V.scalar_tensor_tensor(r, turns[:, :], -C1, angle[:, :], ALU.mult, ALU.add))
                    trig_link(V.scalar_tensor_tensor(r, turns[:, :], -C2, r, ALU.mult, ALU.add))
                    trig_link(V.scalar_tensor_tensor(r, turns[:, :], -C3, r, ALU.mult, ALU.add))
                    trig_link(V.tensor_scalar(r, r, s * np.pi / 2, PI_IN, ALU.add, ALU.min))
                    V.tensor_scalar(r, r, -PI_IN, None, ALU.max).then_inc(trig_ready, 1)
                assert step[0] == 14
                norm(N_X, x_ss[:, :], D)
                with dve.Fori(0, KD_ // 2) as i:
                    dve.wait_ge(bc_ready, c * NORMS + N_X + 1)
                    for n in range(2):
                        dve.wait_ge(h_loaded, c * KD_ + 2 * i + (n + 1))
                        V.scalar_tensor_tensor(u_tmp[:, n], h[:, 2 * i + n], column("g_pre_mix", 2 * i + n), ps[:, BC],
                                               ALU.mult, ALU.mult).then_inc(ut_ready, 1)
                    for n in range(2):
                        dve.wait_ge(u_hi_ready, c * KD_ + 2 * i + (n + 1))
                        V.tensor_tensor(u_lo[:, 2 * i + n], u_tmp[:, n], u_hi[:, 2 * i + n].bitcast(F32),
                                        ALU.subtract).then_inc(u_ready, 1)
                    dve.wait_ge(u_ready, c * KD_ + 2 * i + 2)

                def tap(j, t, count):
                    src = conv_in[:, ds(j, 1), t:t + T].rearrange("p o t -> p (o t)")
                    dst = conv_acc[:, ds(j, 1)].rearrange("p o t -> p (o t)")
                    if t == 0:
                        V.tensor_scalar(dst, src, column("conv_w", j * TAPS), column("conv_b", j),
                                        ALU.mult, ALU.add).then_inc(conv_tap, 1)
                    else:
                        dve.wait_ge(conv_tap, c * (NC * TAPS) + count)
                        V.scalar_tensor_tensor(dst, src, column("conv_w", j * TAPS + t), dst, ALU.mult,
                                               ALU.add).then_inc(conv_tap, 1)

                dve.wait_ge(glu_sig, c * NC + 1)
                V.tensor_copy(conv_in[:, :, 0:HALO], conv_halo[:, :, :]).then_inc(halo_in, 1)
                with dve.Fori(0, NC // 2) as i:
                    dve.wait_ge(halo_in, c + 1)
                    for n in range(2):
                        dve.wait_ge(glu_sig, c * NC + 2 * i + (n + 1))
                        V.tensor_tensor(conv_in[:, 2 * i + n, HALO:], ps[:, 4 * i + 2 * n], glu_sg[:, n], ALU.mult).then_inc(glu_done, 1)
                        dve.wait_ge(glu_done, c * NC + 2 * i + (n + 3))
                        for t in range(EARLY):
                            tap(2 * i + n, t, (2 * i + n) * EARLY + t)
                    dve.wait_ge(conv_tap, c * (NC * TAPS) + (2 * i + 2) * EARLY)
                dve.wait_ge(trig_done, c * 2 + 2)
                V.tensor_copy(k_dup[:, :, 0:CH], k_dup[:, :, T:T + CH]).then_inc(k_halo, 1)
                dve.wait_ge(k_halo, c + 1)
                for j in range(PAIRS + 1):
                    at = (c * (PAIRS + 1) + j) * 2
                    done(B_QKV + j)
                    dve.wait_ge(rope_swapped, c * (PAIRS + 1) + j + 1)
                    V.tensor_tensor(rope_a[:, j % 2], ps[:, QK_BANK[j]], cos_t[:, :], ALU.mult).then_inc(rope_step, 1)
                    V.tensor_tensor(rope_b[:, j % 2], rope_b[:, j % 2], sin_t[:, :], ALU.mult).then_inc(rope_step, 1)
                    dve.wait_ge(rope_step, at + 2)
                    if j < PAIRS:
                        V.tensor_tensor(qT[:, j], rope_a[:, j % 2], rope_b[:, j % 2], ALU.add).then_inc(rope_done, 1)
                    else:
                        for g in range(2):
                            for to in range(2):
                                last = V.tensor_tensor(k_dup[CH * to:CH * to + CH, g, CH:], rope_a[CH * g:CH * g + CH, j % 2],
                                                       rope_b[CH * g:CH * g + CH, j % 2], ALU.add)
                        last.then_inc(rope_done, 1)
                    dve.wait_ge(rope_done, c * (PAIRS + 1) + j + 1)
                dve.wait_ge(v_ready, c + 1)
                V.memset(q_diag[:, :, :, :], 0.0).then_inc(q_zeroed, 1)
                with dve.Fori(0, SUB // 2) as i:
                    step = [0]

                    def link(ins, wait=True):
                        step[0] += 1
                        ins.then_inc(sm_step, 1)
                        if wait:
                            dve.wait_ge(sm_step, c * (SUB // 2 * 10) + i * 10 + step[0])

                    for s in range(2):
                        scores = four(ps[:, ATT + s])
                        dve.wait_ge(qk_done, c * SUB + 2 * i + (s + 1))
                        if s == 0:
                            link(V.tensor_tensor(scores[:, :, CH:], scores[:, :, CH:],
                                                 prev_bias[:, :].unsqueeze(1).broadcast_to([P, PAIRS, CH]), ALU.add))
                            V.memset(prev_bias[:, :], 0.0)
                        link(V.tensor_reduce(s_max[:, s], scores, AX.X, ALU.max))
                        link(V.scalar_tensor_tensor(s_m[:, s], s_max[:, s], SCALE, column_range("sinks"), ALU.mult, ALU.max))
                        V.tensor_tensor(s_sink[:, s], column_range("sinks"), s_m[:, s], ALU.subtract)
                        V.tensor_scalar(s_neg[:, s], s_m[:, s], -1.0, None, ALU.mult).then_inc(sm_ready, 1)
                    for t in range(LATE // 2):
                        tap(i, EARLY + t, NC * EARLY + i * LATE + t)
                    for s in range(2):
                        dve.wait_ge(exp_done, c * SUB + 2 * i + (s + 1))
                        link(V.tensor_tensor(s_den[:, s], s_den[:, s], s_sinke[:, s], ALU.add))
                        link(V.reciprocal(s_rec[:, s], s_den[:, s]))
                        V.tensor_tensor(prob[:, s], prob[:, s], s_rec[:, s].unsqueeze(2).broadcast_to([P, PAIRS, P]),
                                        ALU.mult).then_inc(pn_ready, 1)
                    for t in range(LATE // 2, LATE):
                        tap(i, EARLY + t, NC * EARLY + i * LATE + t)
                    link(V.tensor_copy(conv_halo[:, ds(i, 1)], conv_in[:, ds(i, 1), T:]), wait=False)
                    for s in range(2):
                        dve.wait_ge(ao_hi, c * SUB + 2 * i + (s + 1))
                        now = ds(2 * CH * i + CH * s, CH)
                        ao = four(ps[:, PV + s])
                        V.tensor_tensor(ca_lo[0:CH, NC:, now], ao[0:CH, :, 0:CH], ca_hi[0:CH, NC:, now].bitcast(F32), ALU.subtract)
                        V.tensor_tensor(ca_lo[CH:P, NC:, now], ao[CH:P, :, CH:P], ca_hi[CH:P, NC:, now].bitcast(F32),
                                        ALU.subtract).then_inc(ao_lo, 1)
                    assert step[0] == 10, step[0]
                    dve.wait_ge(ao_lo, c * SUB + 2 * i + 4)
                dve.wait_ge(conv_tap, c * (NC * TAPS) + NC * TAPS)
                for j in range(1, NC):
                    V.tensor_tensor(ssum[:, :], conv_acc[:, 0] if j == 1 else ssum[:, :], conv_acc[:, j], ALU.add).then_inc(ln_summed, 1)
                    dve.wait_ge(ln_summed, c * (NC - 1) + j)
                dve.wait_ge(mean_ready, c + 1)
                for j in range(NC):
                    V.scalar_tensor_tensor(conv_acc[:, j], ps[:, BC], -1.0 / CONV, conv_acc[:, j], ALU.mult,
                                           ALU.add).then_inc(ln_centred, 1)
                zero_sum(0)
                for j in range(NC):
                    add_square(Q_LN + j, j % 2, 0)
                norm(N_LN, ps[:, SMALL, 0:TT], CONV)
                dve.wait_ge(bc_ready, c * NORMS + N_LN + 1)
                for j in range(NC):
                    V.scalar_tensor_tensor(conv_acc[:, j], conv_acc[:, j], column("ln_g", j), ps[:, BC], ALU.mult,
                                           ALU.mult).then_inc(ln_scaled, 1)
                for j in range(NC):
                    dve.wait_ge(c_hi, c * NC + j + 1)
                    V.tensor_tensor(ca_lo[:, j], silu_c[:, j % 2], ca_hi[:, j].bitcast(F32), ALU.subtract).then_inc(c_lo, 1)
                with dve.Fori(0, KD_ // 2) as i:
                    for n in range(2):
                        item = c * KD_ + 2 * i + (n + 1)
                        done(B_MRG + 4 * i + 2 + n)
                        V.tensor_tensor(part_a[:, n], ps[:, 2 * n + 1], gate_a[:, 2 * i + n], ALU.mult).then_inc(part_a_ready, 1)
                        dve.wait_ge(gate_b_ready, item)
                        V.tensor_tensor(part_b[:, n], ps[:, ATT + n], gate_b[:, n], ALU.mult).then_inc(merged, 1)
                        dve.wait_ge(part_a_ready, item)
                        dve.wait_ge(merged, item + 2)
                        V.tensor_tensor(y_tmp[:, n], part_a[:, n], part_b[:, n], ALU.add).then_inc(yt_ready, 1)
                        dve.wait_ge(y_hi_ready, item)
                        V.tensor_tensor(y_lo[:, 2 * i + n], y_tmp[:, n], y_hi[:, 2 * i + n].bitcast(F32),
                                        ALU.subtract).then_inc(y_lo_ready, 1)
                    dve.wait_ge(y_lo_ready, c * KD_ + 2 * i + 2)
                zero_sum(1)
                with dve.Fori(0, KD_ // 2) as i:
                    for n in range(2):
                        add_square(Q_POST + 2 * i + n, n, 1)
                    dve.wait_ge(ss_added, c * NQ + 2 * i + (Q_POST + 4))
                norm(N_POST, ps[:, SMALL, 0:TT], D)
                zero_sum(2)
                with dve.Fori(0, KD_ // 2) as i:
                    dve.wait_ge(bc_ready, c * NORMS + N_POST + 1)
                    for n in range(2):
                        item = c * KD_ + 2 * i + (n + 1)
                        V.scalar_tensor_tensor(h_tmp[:, n], acc[:, 2 * i + n], column("g_post_mix", 2 * i + n), ps[:, BC],
                                               ALU.mult, ALU.mult).then_inc(mid_step, 1)
                        dve.wait_ge(mid_step, item)
                        V.tensor_tensor(h[:, 2 * i + n], h[:, 2 * i + n], h_tmp[:, n], ALU.add).then_inc(h_mid, 1)
                    for n in range(2):
                        item = c * KD_ + 2 * i + (n + 1)
                        dve.wait_ge(u2_hi, item)
                        V.scalar_tensor_tensor(y_lo[:, 2 * i + n], h[:, 2 * i + n], column("g_pre_ffn", 2 * i + n),
                                               y_hi[:, 2 * i + n].bitcast(F32), ALU.mult, ALU.subtract).then_inc(u2_lo, 1)
                    for n in range(2):
                        add_square(Q_PRE + 2 * i + n, n, 2)
                    dve.wait_ge(ss_added, c * NQ + 2 * i + (Q_PRE + 4))
                norm(N_PRE, ps[:, SMALL, 0:TT], D)

                def up(i, first_block, first_tile, banks=(0, 2)):
                    together = first_tile == 0 and isinstance(i, int) and i == 0
                    if not together:
                        dve.wait_ge(f_lo_ready, c * NF + 2 * i + first_tile)
                    for n in range(2):
                        item = c * NF + 2 * i + (first_tile + n + 1)
                        at = (c * NF + 2 * i + (first_tile + n)) * 3
                        halo = ffn_halo[:, 2 * i + (first_tile + n)]
                        slot = 2 * i + (first_tile % F1 + n)

                        def value():
                            done(first_block + (3 if together else 4 * i + 2 * n + 1))
                            V.tensor_tensor(f_val[:, n], ps[:, banks[n] + 1], r_ffn[:, :], ALU.mult).then_inc(val_read, 1)

                        done(first_block + (3 if together else 4 * i + 2 * n))
                        V.tensor_copy(g_in[:, n, 0:2], halo).then_inc(ffn_step, 1)
                        V.tensor_tensor(g_in[:, n, 2:], ps[:, banks[n]], r_ffn[:, :], ALU.mult).then_inc(ffn_step, 1)
                        dve.wait_ge(ffn_step, at + 2)
                        V.tensor_scalar(halo, g_in[:, n, T:], 1.0, None, ALU.mult).then_inc(g_in_ready, 1)
                        if together:
                            value()
                        dve.wait_ge(tap0_ready, item)
                        V.scalar_tensor_tensor(g_conv[:, n], g_in[:, n, 1:T + 1], column("ffn_w", 6 * i + (3 * (first_tile + n) + 1)),
                                               g_conv[:, n], ALU.mult, ALU.add).then_inc(ffn_step, 1)
                        dve.wait_ge(ffn_step, at + 3)
                        V.scalar_tensor_tensor(g_conv[:, n], g_in[:, n, 2:], column("ffn_w", 6 * i + (3 * (first_tile + n) + 2)),
                                               g_conv[:, n], ALU.mult, ALU.add).then_inc(conv3_done, 1)
                        if not together:
                            value()
                        dve.wait_ge(val_read, item + 2)
                        dve.wait_ge(gelu_ready, item)
                        V.tensor_tensor(f_tmp[:, n], g_act[:, n], f_val[:, n], ALU.mult).then_inc(ft_ready, 1)
                        dve.wait_ge(f_hi_ready, item)
                        V.tensor_tensor(f_lo[:, slot], f_tmp[:, n], f_hi[:, slot].bitcast(F32),
                                        ALU.subtract).then_inc(f_lo_ready, 1)

                dve.wait_ge(r_ffn_ready, c + 1)
                up(0, B_UP1, 0)
                up(1, B_UP1, 0, banks=(4, 2))
                with dve.Fori(2, F1 // 2) as i:
                    up(i, B_UP1, 0)
                for k in range(NP):
                    dve.wait_ge(p_hi, c * NP + k + 1)
                    V.tensor_tensor(f_lo[:, F1 - NP + k], ps[:, ATT + k], f_hi[:, F1 - NP + k].bitcast(F32),
                                    ALU.subtract).then_inc(p_lo, 1)
                with dve.Fori(0, F2 // 2) as i:
                    up(i, B_UP2, F1)
                zero_sum(3)
                for j in range(KD_):
                    done(B_DN2 + (F2 * (j + 1) - 1) // 8)
                    V.tensor_tensor(acc[:, j], acc[:, j], ps[:, j % 4], ALU.add).then_inc(d2_acc, 1)
                    if j >= 1:
                        add_square(Q_PF + j - 1, (j - 1) % 2, 3)
                add_square(Q_PF + KD_ - 1, (KD_ - 1) % 2, 3)
                norm(N_PF, ps[:, SMALL, 0:TT], D)
                with dve.Fori(0, KD_ // 2) as i:
                    dve.wait_ge(bc_ready, c * NORMS + N_PF + 1)
                    for n in range(2):
                        item = c * KD_ + 2 * i + (n + 1)
                        V.scalar_tensor_tensor(h_tmp[:, n], acc[:, 2 * i + n], column("g_post_ffn", 2 * i + n), ps[:, BC],
                                               ALU.mult, ALU.mult).then_inc(h3_step, 1)
                        dve.wait_ge(h3_step, item)
                        V.tensor_tensor(h[:, 2 * i + n], h[:, 2 * i + n], h_tmp[:, n], ALU.add).then_inc(h3_mid, 1)
                    for n in range(2):
                        item = c * KD_ + 2 * i + (n + 1)
                        dve.wait_ge(h3_hi, item)
                        V.tensor_tensor(y_lo[:, 2 * i + n], h[:, 2 * i + n], y_hi[:, 2 * i + n].bitcast(F32),
                                        ALU.subtract).then_inc(h3_lo, 1)
                    dve.wait_ge(h3_lo, c * KD_ + 2 * i + 3)
                with dve.Fori(0, KD_ // 2) as i:
                    dve.wait_ge(ple_out, c * KD_ + KD_)
                    for n in range(2):
                        item = c * KD_ + 2 * i + (n + 1)
                        dve.wait_ge(ple_sig, item + 2)
                        V.tensor_tensor(ple_t[:, n], ple[:, 2 * i + n], ple_sg[:, n], ALU.mult).then_inc(ple_mul, 1)
                        dve.wait_ge(ple_mul, item)
                        V.tensor_tensor(h[:, 2 * i + n], h[:, 2 * i + n], ple_t[:, n], ALU.add).then_inc(out_ready, 1)
                    dve.wait_ge(out_ready, c * KD_ + 2 * i + 4)



def _tiles(w, rows, cols):
    return [w[r * P:(r + 1) * P, n * P:(n + 1) * P] for r, n in zip(rows, cols)]


def weight_stream(w_in, w_conv_out, w_attn_out, w_out, w_up, w_down, w_ple, w_ple_gate):
    tiles = []

    def column_of(w, n, rows=None):
        tiles.extend(_tiles(w, rows or range(w.shape[0] // P), [n] * (len(rows) if rows else w.shape[0] // P)))

    def four_by_tile(w, columns):
        for k in range(8):
            for n in columns:
                tiles.extend(_tiles(w, [k], [n]))

    def pairs(w, js, second):
        for j in js:
            column_of(w, j)
            column_of(w, second + j)

    four_by_tile(w_in, (0, NC, 1, NC + 1))
    pairs(w_in, range(2, NC), NC)
    first = 2 * NC
    for j in range(PAIRS + 2):
        column_of(w_in, first + j)
    first += PAIRS + 2
    for j in range(KD_):
        column_of(w_in, first + j)
    for j in range(0, KD_, 2):
        column_of(w_in, first + KD_ + j)
        column_of(w_in, first + KD_ + j + 1)
        for n in range(2):
            column_of(w_conv_out, j + n)
            column_of(w_attn_out, j + n)
    for j in range(KD_):
        column_of(w_out, j)
    four_by_tile(w_up, (0, NF, 1, NF + 1))
    pairs(w_up, range(2, F1), NF)
    for j in range(KD_):
        column_of(w_down, j, list(range(F1)))
    pairs(w_up, range(F1, NF), NF)
    for j in range(KD_):
        column_of(w_down, j, list(range(F1, NF)))
    for j in range(KD_):
        column_of(w_ple, j)
    four_by_tile(w_ple_gate, range(4))
    for j in range(4, KD_):
        column_of(w_ple_gate, j)
    stream = np.stack(tiles).reshape(NB, 8, P, P)
    return np.ascontiguousarray(stream.transpose(0, 2, 1, 3)).reshape(NB, P, 8 * P)


def column_array(g_pre_mix, conv_dw_w, conv_dw_b, conv_ln_g, conv_ln_b, g_post_mix, g_pre_ffn, ffn_dw_w, ffn_dw_b,
                 g_post_ffn, attn_sinks):
    def cols(v):
        return v.reshape(-1, P).T

    def taps(w):
        return w.T.reshape(-1, P, w.shape[0]).transpose(1, 0, 2).reshape(P, -1)

    half = HD // 2
    inv_freq = (10000.0 ** (-np.arange(half) / half)).astype(np.float32)
    sign = np.where(np.arange(P) % HD < half, -1.0, 1.0).astype(np.float32)
    parts = {
        "g_pre_mix": cols(g_pre_mix), "conv_w": taps(conv_dw_w), "conv_b": cols(conv_dw_b), "ln_g": cols(conv_ln_g),
        "ln_b": cols(conv_ln_b), "g_post_mix": cols(g_post_mix), "g_pre_ffn": cols(g_pre_ffn), "ffn_w": taps(ffn_dw_w),
        "ffn_b": cols(ffn_dw_b), "g_post_ffn": cols(g_post_ffn),
        "sinks": np.repeat(attn_sinks.reshape(PAIRS, 2).T, CH, axis=0),
        "inv_freq": np.tile(inv_freq, P // half)[:, None], "sin_sign": sign[:, None],
        "eps": np.full((P, 1), EPS, np.float32),
    }
    return np.ascontiguousarray(np.concatenate([parts[n] for n in COLS], axis=1))


def kernel(x, p, positions, g_pre_mix, w_in, conv_dw_w, conv_dw_b, conv_ln_g, conv_ln_b, w_conv_out, attn_sinks,
           w_attn_out, w_out, g_post_mix, g_pre_ffn, w_up, ffn_dw_w, ffn_dw_b, w_down, g_post_ffn, w_ple, w_ple_gate):
    import concourse.bacc as bacc
    from concourse.bass_utils import run_bass_kernel_spmd

    n = {k: np.asarray(v) for k, v in locals().items() if k not in ("bacc", "run_bass_kernel_spmd")}
    arrays = {
        "x": np.ascontiguousarray(n["x"][0]),
        "p": np.ascontiguousarray(n["p"][0, 0]),
        "positions": np.ascontiguousarray(n["positions"]),
        "weights": weight_stream(*(n[k][0] for k in ("w_in", "w_conv_out", "w_attn_out", "w_out", "w_up", "w_down",
                                                     "w_ple", "w_ple_gate"))),
        "columns": column_array(*(n[k][0] for k in ("g_pre_mix", "conv_dw_w", "conv_dw_b", "conv_ln_g", "conv_ln_b",
                                                    "g_post_mix", "g_pre_ffn", "ffn_dw_w", "ffn_dw_b", "g_post_ffn",
                                                    "attn_sinks"))),
        "identity": np.eye(P, dtype=np.float32),
    }
    nc = bacc.Bacc("TRN2", target_bir_lowering=False, num_devices=1, dynamic_dma_scratch_size=1024)
    args = {k: nc.dram_tensor(f"in_{k}", a.shape, mybir.dt.from_np(a.dtype), kind="ExternalInput").ap()
            for k, a in arrays.items()}
    out = nc.dram_tensor("out_h", (SEQ, D), F32, kind="ExternalOutput").ap()
    build_kernel(nc, out=out, **args)
    got = run_bass_kernel_spmd(nc, [{f"in_{k}": a for k, a in arrays.items()}], core_ids=[0])
    return got.results[0]["out_h"].reshape(1, SEQ, D)
```

```python
from contextlib import ExitStack

import numpy as np

import concourse.bass as bass
from concourse import mybir

F32 = mybir.dt.float32
F32R = mybir.dt.float32r
I32 = mybir.dt.int32
ALU = mybir.AluOpType
ACT = mybir.ActivationFunctionType
AX = mybir.AxisListType
ds = bass.ds

P = 128
D = 1024
SEQ = 2048
T = 512
CHUNKS = SEQ // T
TT = T // P
KD_ = D // P
CONV = 512
NC = CONV // P
TAPS = 31
HALO = TAPS - 1
EARLY = 15
LATE = TAPS - EARLY
TAPS_A, TAPS_B = 6, 10
HEADS = 8
HD = 64
PAIRS = HEADS // 2
CH = 64
SUB = T // CH
FF = 2816
NF = FF // P
F1 = 16
F2 = NF - F1
PLE = 256
NP = PLE // P
EPS = 1e-6
SCALE = HD ** -0.5

SLOTS = 2
B_GLU = 0
B_QKV = B_GLU + 2 * NC
B_GA = B_QKV + PAIRS + 2
B_MRG = B_GA + KD_
B_WO = B_MRG + 2 * KD_
B_UP1 = B_WO + KD_
B_DN1 = B_UP1 + 2 * F1
B_UP2 = B_DN1 + 2 * KD_
B_DN2 = B_UP2 + 2 * F2
B_WP = B_DN2 + F2 * KD_ // 8
B_PG = B_WP + NP * KD_ // 8
NB = B_PG + KD_
assert NB == 122 and all(b % 2 == 0 for b in (B_QKV, B_GA, B_MRG, B_WO, B_UP1, B_DN1, B_UP2, B_DN2, B_WP, B_PG, NB))

COLS = {}


def _col(name, n):
    COLS[name] = sum(w for _, w in COLS.values()), n


for _name, _n in (("g_pre_mix", KD_), ("conv_w", NC * TAPS), ("conv_b", NC), ("ln_g", NC), ("ln_b", NC),
                  ("g_post_mix", KD_), ("g_pre_ffn", KD_), ("ffn_w", NF * 3), ("ffn_b", NF), ("g_post_ffn", KD_),
                  ("sinks", PAIRS), ("inv_freq", 1), ("sin_sign", 1), ("eps", 1)):
    _col(_name, _n)
NCOL = sum(w for _, w in COLS.values())

N_X, N_LN, N_POST, N_PRE, N_PF = range(5)
NORMS = 5
Q_LN, Q_POST, Q_PRE, Q_PF = 0, NC, NC + KD_, NC + 2 * KD_
NQ = NC + 3 * KD_

TWO_PI = 2 * np.pi
C1 = 6.28125
C2 = float(np.floor((TWO_PI - C1) * 2 ** 20) / 2 ** 20)
C3 = float(np.float32(TWO_PI - C1 - C2))
MAGIC = 1.5 * 2 ** 23
PI_IN = 3.1415925


def build_kernel(nc, x, p, positions, weights, columns, identity, out):
    with ExitStack() as ctx:
        top = [(nc.sbuf_base + 63) // 64 * 64]

        def region(nbytes):
            at = top[0]
            top[0] += (nbytes + 63) // 64 * 64
            assert top[0] <= nc.sbuf_usable_end, top[0]
            return at

        def sb(name, shape, dt, at=None):
            n = 4 * int(np.prod(shape[1:]))
            return nc.alloc_sbuf_tensor_at(name, shape, dt, offset=region(n) if at is None else at)

        K = 1024
        w_stage = sb("w_stage", [P, SLOTS, 8, P], F32)
        w_hi = sb("w_hi", [P, SLOTS, 8, P], F32R)
        w_lo = sb("w_lo", [P, SLOTS, 8, P], F32R)
        at = region(64 * K)
        u_hi = sb("u_hi", [P, KD_, T], F32R, at)
        u_lo = sb("u_lo", [P, KD_, T], F32R, at + 16 * K)
        ca_hi = sb("ca_hi", [P, KD_, T], F32R, at + 32 * K)
        ca_lo = sb("ca_lo", [P, KD_, T], F32R, at + 48 * K)
        f_hi = sb("f_hi", [P, F1, T], F32R, at)
        f_lo = sb("f_lo", [P, F1, T], F32R, at + 32 * K)
        y_hi = sb("y_hi", [P, KD_, T], F32R)
        y_lo = sb("y_lo", [P, KD_, T], F32R)
        h = sb("h", [P, KD_, T], F32)
        at = region(16 * K)
        x_rows = sb("x_rows", [P, TT, D], F32, at)
        gate_a = sb("gate_a", [P, KD_, T], F32, at)
        acc = sb("acc", [P, KD_, T], F32, at)
        at = region(4 * (NC * (HALO + T) + NC * T))
        conv_in = sb("conv_in", [P, NC, HALO + T], F32, at)
        conv_acc = sb("conv_acc", [P, NC, T], F32, at + 4 * NC * (HALO + T))
        p_rows = sb("p_rows", [P, TT, PLE], F32, at)
        ple = sb("ple", [P, KD_, T], F32, at)
        conv_halo = sb("conv_halo", [P, NC, HALO], F32)
        ffn_halo = sb("ffn_halo", [P, NF, 2], F32)
        k_dup = sb("k_dup", [P, 2, CH + T], F32)
        v_odd = sb("v_odd", [P, TT, P], F32)
        v_even = sb("v_even", [P, TT + 1, P], F32)
        at = region(22 * K)
        junk = sb("junk", [P, D], F32, at + 8 * K)
        u_tmp = sb("u_tmp", [P, 2, T], F32, at + 4 * K)
        qT = sb("qT", [P, PAIRS, T], F32, at)
        cos_t = sb("cos_t", [P, T], F32, at + 8 * K)
        sin_t = sb("sin_t", [P, T], F32, at + 10 * K)
        angle = sb("angle", [P, T], F32, at + 14 * K)
        turns = sb("turns", [P, T], F32, at + 16 * K)
        trig = sb("trig", [P, 2, T], F32, at + 18 * K)
        glu_sg = sb("glu_sg", [P, 2, T], F32, at + 12 * K)
        rope_a = sb("rope_a", [P, 2, T], F32, at + 12 * K)
        rope_b = sb("rope_b", [P, 2, T], F32, at + 16 * K)
        prob = sb("prob", [P, 2, PAIRS, P], F32, at + 8 * K)
        probT = sb("probT", [P, 2, PAIRS, P], F32, at + 12 * K)
        v_cur = sb("v_cur", [P, 2, 2, 2, HD], F32, at + 16 * K)
        q_diag = sb("q_diag", [P, 2, PAIRS, P], F32, at + 18 * K)
        silu_c = sb("silu_c", [P, 2, T], F32, at + 8 * K)
        gate_b = sb("gate_b", [P, 2, T], F32, at)
        part_a = sb("part_a", [P, 2, T], F32, at + 4 * K)
        part_b = sb("part_b", [P, 2, T], F32, at + 8 * K)
        y_tmp = sb("y_tmp", [P, 2, T], F32, at + 12 * K)
        h_tmp = sb("h_tmp", [P, 2, T], F32, at + 12 * K)
        g_in = sb("g_in", [P, 2, 2 + T], F32, at)
        g_conv = sb("g_conv", [P, 2, T], F32, at + 4 * K + 64)
        g_act = sb("g_act", [P, 2, T], F32, at + 8 * K + 64)
        f_val = sb("f_val", [P, 2, T], F32, at + 12 * K + 64)
        f_tmp = sb("f_tmp", [P, 2, T], F32, at + 16 * K + 64)
        ple_sg = sb("ple_sg", [P, 2, T], F32, at)
        ple_t = sb("ple_t", [P, 2, T], F32, at + 4 * K)
        pos_i = sb("pos_i", [P, T], I32)
        ssum = sb("ssum", [P, T], F32)
        sq = sb("sq", [P, 2, T], F32)
        diag = sb("diag", [P, TT, P], F32)
        r_ffn = sb("r_ffn", [P, T], F32)
        ident = sb("ident", [P, P], F32)
        ones = sb("ones", [P, P], F32)
        col = sb("col", [P, NCOL], F32)
        prev_bias = sb("prev_bias", [P, CH], F32)
        x_ss = sb("x_ss", [P, TT], F32)
        n_root = sb("n_root", [P, TT], F32)
        n_var = sb("n_var", [P, TT], F32)
        n_r = sb("n_r", [P, TT], F32)
        n_t = sb("n_t", [P, TT], F32)
        s_max = sb("s_max", [P, 2, PAIRS], F32)
        s_m = sb("s_m", [P, 2, PAIRS], F32)
        s_neg = sb("s_neg", [P, 2, PAIRS], F32)
        s_sink = sb("s_sink", [P, 2, PAIRS], F32)
        s_sinke = sb("s_sinke", [P, 2, PAIRS], F32)
        s_den = sb("s_den", [P, 2, PAIRS], F32)
        s_rec = sb("s_rec", [P, 2, PAIRS], F32)

        ps = ctx.enter_context(nc.psum_tensor("ps", [P, 8, T], F32))
        SMALL, BC = 6, 7
        XT_BANK = 2
        QK_BANK = 2, 3, 0, 1, 4
        V_BANK = 5
        GA_BANK = 2
        SC = 0
        PV = 6
        GB_BANK, CV_BANK, AT_BANK = (0, 2), (1, 3), (4, 5)
        WO_BANK = 0, 2, 6, 7, 1, 3, 4, 5
        DN1_BANK = 4
        DN2_BANK = 4, 5, 0, 1
        PLE_BANK = 2, 3, 4, 5, 0, 1, 2, 3
        PG_BANK = 4, 5, 0, 1, 2, 3, 4, 5
        OT_BANK = 6, 7, 0, 1

        def column(name, i=0):
            first, n = COLS[name]
            return col[:, ds(first + i, 1)] if not isinstance(i, int) else col[:, first + i:first + i + 1]

        def column_range(name):
            first, n = COLS[name]
            return col[:, first:first + n]

        def four(ap):
            return ap.rearrange("p (t n) -> p t n", t=TT)

        def sem(name):
            return ctx.enter_context(nc.semaphore(name))

        const_loaded, x_loaded, pos_loaded, p_loaded, out_stored = map(
            sem, ("const_loaded", "x_loaded", "pos_loaded", "p_loaded", "out_stored"))
        w_loaded = [sem("w_loaded_even"), sem("w_loaded_odd")]
        setup = sem("setup")
        block_done = sem("block_done")
        w_hi_ready = sem("w_hi_ready")
        w_lo_ready = sem("w_lo_ready")
        x_squared = sem("x_squared")
        xt_done, h_loaded, ut_ready, u_hi_ready, u_ready = map(
            sem, ("xt_done", "h_loaded", "ut_ready", "u_hi_ready", "u_ready"))
        root_ready, norm_step, diag_ready, bc_ready = map(sem, ("root_ready", "norm_step", "diag_ready", "bc_ready"))
        sq_ready, ss_added, ss_zeroed, ssum_done = map(sem, ("sq_ready", "ss_added", "ss_zeroed", "ssum_done"))
        trig_step, trig_ready, trig_done = map(sem, ("trig_step", "trig_ready", "trig_done"))
        glu_sig, glu_done, halo_in, conv_tap = map(sem, ("glu_sig", "glu_done", "halo_in", "conv_tap"))
        rope_swapped, rope_step, rope_done, k_halo, v_step, v_ready = map(
            sem, ("rope_swapped", "rope_step", "rope_done", "k_halo", "v_step", "v_ready"))
        q_diag_ready, q_zeroed, v_cur_ready, qk_done, sm_step, sm_ready, exp_done, pn_ready, t_done, pt_ready, pv_done, \
            ao_hi, ao_lo, gate_a_ready = map(sem, (
                "q_diag_ready", "q_zeroed", "v_cur_ready", "qk_done", "sm_step", "sm_ready", "exp_done", "pn_ready", "t_done",
                "pt_ready", "pv_done", "ao_hi", "ao_lo", "gate_a_ready"))
        ln_summed, mean_ready, ln_centred, ln_scaled, silu_ready, c_hi, c_lo = map(
            sem, ("ln_summed", "mean_ready", "ln_centred", "ln_scaled", "silu_ready", "c_hi", "c_lo"))
        gate_b_ready, part_a_ready, merged, yt_ready, y_hi_ready, y_lo_ready, y2_out = map(
            sem, ("gate_b_ready", "part_a_ready", "merged", "yt_ready", "y_hi_ready", "y_lo_ready", "y2_out"))
        mid_step, h_mid, u2_hi, u2_lo, r_ffn_ready = map(sem, ("mid_step", "h_mid", "u2_hi", "u2_lo", "r_ffn_ready"))
        ffn_step, g_in_ready, tap0_ready, conv3_done, gelu_ready, val_read, ft_ready, f_hi_ready, f_lo_ready = map(
            sem, ("ffn_step", "g_in_ready", "tap0_ready", "conv3_done", "gelu_ready", "val_read", "ft_ready",
                  "f_hi_ready", "f_lo_ready"))
        d1_out, d2_acc, pt_done, p_hi, p_lo, ple_out = map(sem, ("d1_out", "d2_acc", "pt_done", "p_hi", "p_lo", "ple_out"))
        pn_step = sem("pn_step")
        h3_step, h3_mid, h3_hi, h3_lo, ple_sig, ple_mul, out_ready, ot_done, os_out = map(
            sem, ("h3_step", "h3_mid", "h3_hi", "h3_lo", "ple_sig", "ple_mul", "out_ready", "ot_done", "os_out"))
        SETUPS = 7

        block = ctx.enter_context(nc.Block())

        @block.sync
        def _(sp):
            sp.dma_start(col[:, :], columns).then_inc(const_loaded, 16)
            sp.dma_start(ident[:, :], identity).then_inc(const_loaded, 16)

            def load_x(token):
                sp.dma_start(x_rows[:, :, :], x[ds(token, T), :].rearrange("(t p) d -> p t d", p=P)).then_inc(x_loaded, 16)

            def load_positions(token):
                sp.dma_start(pos_i[:, :], positions[0:1, ds(token, T)].broadcast_to([P, T])).then_inc(pos_loaded, 16)

            load_x(0)
            load_positions(0)
            with sp.Fori(0, CHUNKS) as c:
                def load_blocks(first, count):
                    with sp.Fori(0, count // 2) as i:
                        for par in range(2):
                            sp.wait_ge(w_lo_ready, c * NB + 2 * i + (first + par + 1))
                            sp.dma_start(w_stage[:, par].rearrange("p k n -> p (k n)"),
                                         weights[2 * i + (first + par)]).then_inc(w_loaded[par], 16)

                load_blocks(0, B_UP1)
                sp.wait_ge(c_lo, c * NC + NC)
                sp.dma_start(p_rows[:, :, :], p[ds(c * T, T), :].rearrange("(t p) d -> p t d", p=P)).then_inc(p_loaded, 16)
                load_positions(((c + 1) & (CHUNKS - 1)) * T)
                load_blocks(B_UP1, NB - B_UP1)
                load_x(((c + 1) & (CHUNKS - 1)) * T)

        @block.gpsimd
        def _(pool):
            pool.sem_inc(w_lo_ready, SLOTS)
            with pool.Fori(0, CHUNKS * NB // 2) as i:
                for par in range(2):
                    pool.wait_ge(w_hi_ready, 2 * i + (par + 1))
                    nc.gpsimd.tensor_tensor(w_lo[:, par], w_stage[:, par], w_hi[:, par].bitcast(F32),
                                            ALU.subtract).then_inc(w_lo_ready, 1)

        @block.scalar
        def _(act):
            copy = nc.scalar.activation
            act.sem_inc(out_stored, 16 * KD_)
            act.sem_inc(gate_a_ready, 2)
            act.sem_inc(y2_out, 4)
            act.sem_inc(d1_out, 2)
            act.sem_inc(ple_sig, 2)
            act.sem_inc(os_out, 4)
            act.wait_ge(const_loaded, 32)
            act.wait_ge(setup, SETUPS)

            def x_square(c, t):
                if t == 0:
                    act.wait_ge(x_loaded, c * 16 + 16)
                copy(junk[:, :], x_rows[:, t], ACT.Square, accum_out=x_ss[:, t:t + 1]).then_inc(x_squared, 1)
                act.wait_ge(x_squared, c * TT + t + 1)

            def root(src, count):
                copy(n_root[:, :], src, ACT.Sqrt, bias=column("eps"), scale=1.0 / count).then_inc(root_ready, 1)

            for t in range(TT):
                x_square(0, t)
            root(x_ss[:, :], D)
            with act.Fori(0, CHUNKS) as c:
                def split(half, par):
                    act.wait_ge(block_done, c * NB + 2 * half + (par + 1))
                    act.wait_ge(w_loaded[par], (c * (NB // 2) + half + 1) * 16)
                    copy(w_hi[:, par], w_stage[:, par], ACT.Copy).then_inc(w_hi_ready, 1)

                def split_block(b):
                    split(b // 2, b % 2)

                def done(b):
                    act.wait_ge(block_done, c * NB + b + (1 + SLOTS))

                def square(q, src, slot):
                    act.wait_ge(ss_added, c * NQ + q + 1)
                    copy(sq[:, slot], src, ACT.Square).then_inc(sq_ready, 1)

                split(0, 0)
                split(0, 1)
                def u_tiles(i):
                    for n in range(2):
                        act.wait_ge(ut_ready, c * KD_ + 2 * i + (n + 1))
                        copy(u_hi[:, 2 * i + n], u_tmp[:, n], ACT.Copy).then_inc(u_hi_ready, 1)

                with act.Fori(0, 2) as i:
                    u_tiles(i)
                split(B_GLU // 2 + 1, 0)
                u_tiles(2)
                split(B_GLU // 2 + 1, 1)
                u_tiles(3)
                split_block(B_GLU + 4)
                act.wait_ge(trig_ready, c * 2 + 1)
                copy(sin_t[:, :], trig[:, 0], ACT.Sin, scale=column("sin_sign")).then_inc(trig_done, 1)
                act.wait_ge(trig_ready, c * 2 + 2)
                copy(cos_t[:, :], trig[:, 1], ACT.Sin).then_inc(trig_done, 1)
                act.wait_ge(out_stored, c * (16 * KD_) + 16 * KD_)
                split_block(B_GLU + 5)
                for j in range(NC):
                    if j >= 2:
                        split(B_GLU // 2 + j + 1, 0)
                    done(B_GLU + max(2 * j + 1, 3))
                    act.wait_ge(glu_done, c * NC + j + 1)
                    copy(glu_sg[:, j % 2], ps[:, 2 * j + 1], ACT.Sigmoid).then_inc(glu_sig, 1)
                    if j >= 2:
                        split(B_GLU // 2 + j + 1, 1)
                for j in range(PAIRS + 1):
                    split_block(B_QKV + j + 2)
                    done(B_QKV + j)
                    if j == 0:
                        act.wait_ge(trig_done, c * 2 + 2)
                    if j >= 2:
                        act.wait_ge(rope_done, c * (PAIRS + 1) + j - 1)
                    for q in range(4):
                        last = copy(rope_b[32 * q:32 * q + 32, j % 2], ps[32 * (q ^ 1):32 * (q ^ 1) + 32, QK_BANK[j]],
                                    ACT.Copy)
                    last.then_inc(rope_swapped, 1)

                def attend_q(i):
                    for s in range(2):
                        now = ds(2 * CH * i + CH * s, CH)
                        copy(q_diag[0:CH, s, :, 0:CH], qT[0:CH, :, now], ACT.Copy)
                        copy(q_diag[CH:P, s, :, CH:P], qT[CH:P, :, now], ACT.Copy).then_inc(q_diag_ready, 1)

                act.wait_ge(rope_done, (c + 1) * (PAIRS + 1))
                act.wait_ge(q_zeroed, c + 1)
                attend_q(0)
                split_block(B_GA + 1)
                done(B_QKV + PAIRS + 1)
                v_new = four(ps[:, V_BANK])
                copy(v_even[CH:P, 0], v_even[CH:P, TT], ACT.Copy)
                copy(v_odd[:, :, :], v_new, ACT.Copy).then_inc(v_step, 1)
                act.wait_ge(v_step, c + 1)
                copy(v_even[0:CH, 0:TT], v_new[0:CH], ACT.Copy)
                copy(v_even[CH:P, 1:TT + 1], v_new[CH:P], ACT.Copy).then_inc(v_ready, 1)
                def attend_exp(i):
                    for s in range(2):
                        act.wait_ge(sm_ready, c * SUB + 2 * i + (s + 1))
                        for a in range(PAIRS):
                            copy(prob[:, s, a], ps[:, SC + s, P * a:P * a + P], ACT.Exp, bias=s_neg[:, s, a:a + 1],
                                 scale=SCALE, accum_out=s_den[:, s, a:a + 1])
                        copy(s_sinke[:, s], s_sink[:, s], ACT.Exp).then_inc(exp_done, 1)

                def attend(i, more):
                    for s, v in enumerate((v_even, v_odd)):
                        src = v[:, ds(i, 1)].rearrange("p o (g d) -> p (o g) d", g=2)
                        for twice in range(2):
                            last = copy(v_cur[:, s, :, twice], src, ACT.Copy)
                        last.then_inc(v_cur_ready, 1)
                    if more:
                        attend_q(i + 1)
                    split(B_GA // 2 + i + 1, 0)
                    split(B_GA // 2 + i + 1, 1)
                    for s in range(2):
                        act.wait_ge(t_done, c * SUB + 2 * i + (s + 1))
                        copy(probT[:, s], four(ps[:, PV + s]), ACT.Copy).then_inc(pt_ready, 1)
                    for s in range(2):
                        copy(gate_a[:, 2 * i + s], ps[:, GA_BANK + s], ACT.Sigmoid).then_inc(gate_a_ready, 1)
                    for s in range(2):
                        act.wait_ge(pv_done, c * SUB + 2 * i + (s + 1))
                        now = ds(2 * CH * i + CH * s, CH)
                        ao = four(ps[:, PV + s])
                        copy(ca_hi[0:CH, NC:, now], ao[0:CH, :, 0:CH], ACT.Copy)
                        copy(ca_hi[CH:P, NC:, now], ao[CH:P, :, CH:P], ACT.Copy).then_inc(ao_hi, 1)
                    if more:
                        attend_exp(i + 1)

                act.wait_ge(v_ready, c + 1)
                attend_exp(0)
                with act.Fori(0, SUB // 2 - 1) as i:
                    attend(i, True)
                attend(SUB // 2 - 1, False)
                def gate_b_tile(i, n):
                    act.wait_ge(merged, c * KD_ + 2 * i + (n + 1))
                    copy(gate_b[:, n], ps[:, GB_BANK[n]], ACT.Sigmoid).then_inc(gate_b_ready, 1)

                def centred_square(j):
                    act.wait_ge(ln_centred, c * NC + j + 1)
                    square(Q_LN + j, conv_acc[:, j], j % 2)

                split_block(B_MRG + 2)
                gate_b_tile(0, 0)
                centred_square(0)
                centred_square(1)
                split_block(B_MRG + 3)
                centred_square(2)
                centred_square(3)
                gate_b_tile(0, 1)
                act.wait_ge(ssum_done, c * (NORMS - 1) + 1)
                root(ps[:, SMALL, 0:TT], CONV)
                split_block(B_MRG + 4)
                for j in range(NC):
                    act.wait_ge(ln_scaled, c * NC + j + 1)
                    if j >= 2:
                        act.wait_ge(c_lo, c * NC + j - 1)
                    copy(silu_c[:, j % 2], conv_acc[:, j], ACT.Silu, bias=column("ln_b", j)).then_inc(silu_ready, 1)
                    act.wait_ge(silu_ready, c * NC + j + 1)
                    copy(ca_hi[:, j], silu_c[:, j % 2], ACT.Copy).then_inc(c_hi, 1)
                    if j == 1:
                        split_block(B_MRG + 5)
                def merge_y(i):
                    for n in range(2):
                        act.wait_ge(yt_ready, c * KD_ + 2 * i + (n + 1))
                        copy(y_hi[:, 2 * i + n], y_tmp[:, n], ACT.Copy).then_inc(y_hi_ready, 1)

                split_block(B_MRG + 6)
                merge_y(0)
                gate_b_tile(1, 0)
                split_block(B_MRG + 7)
                gate_b_tile(1, 1)
                split_block(B_MRG + 8)
                split_block(B_MRG + 9)
                merge_y(1)
                with act.Fori(2, KD_ // 2) as i:
                    for n in range(2):
                        split(B_MRG // 2 + 2 * i + 1, n)
                        gate_b_tile(i, n)
                    for n in range(2):
                        split(B_MRG // 2 + 2 * i + 2, n)
                    merge_y(i)

                def out_projection(j):
                    done(B_WO + max(j, 3))
                    square(Q_POST + j, ps[:, WO_BANK[j]], j % 2)
                    copy(acc[:, j], ps[:, WO_BANK[j]], ACT.Copy).then_inc(y2_out, 1)

                for b in range(2, 6):
                    split_block(B_WO + b)
                act.wait_ge(merged, c * KD_ + (KD_ + 2))
                out_projection(0)
                out_projection(1)
                split_block(B_WO + 6)
                out_projection(2)
                out_projection(3)
                split_block(B_WO + 7)
                out_projection(4)
                out_projection(5)
                split_block(B_UP1)
                out_projection(6)
                out_projection(7)
                split_block(B_UP1 + 1)
                act.wait_ge(ssum_done, c * (NORMS - 1) + 2)
                root(ps[:, SMALL, 0:TT], D)
                def mid_tiles(i):
                    for n in range(2):
                        act.wait_ge(ss_added, c * NQ + Q_PRE + 2 * i + (n + 1))
                        act.wait_ge(h_mid, c * KD_ + 2 * i + (n + 1))
                        copy(y_hi[:, 2 * i + n], h[:, 2 * i + n], ACT.Identity, bias=0.0,
                             scale=column("g_pre_ffn", 2 * i + n)).then_inc(u2_hi, 1)
                        copy(sq[:, n], h[:, 2 * i + n], ACT.Square).then_inc(sq_ready, 1)

                with act.Fori(0, 2) as i:
                    mid_tiles(i)
                split_block(B_UP1 + 2)
                mid_tiles(2)
                split_block(B_UP1 + 3)
                mid_tiles(3)
                split_block(B_UP1 + 4)
                act.wait_ge(ssum_done, c * (NORMS - 1) + 3)
                root(ps[:, SMALL, 0:TT], D)
                act.wait_ge(bc_ready, c * NORMS + N_PRE + 1)
                copy(r_ffn[:, :], ps[:, BC], ACT.Copy).then_inc(r_ffn_ready, 1)
                split_block(B_UP1 + 5)

                def up(i, n, first_block, first_tile, splits=True):
                    item = c * NF + 2 * i + (first_tile + n + 1)
                    if splits:
                        split(first_block // 2 + 2 * i + (n + 1), 0)
                    act.wait_ge(g_in_ready, item)
                    copy(g_conv[:, n], g_in[:, n, 0:T], ACT.Identity, bias=column("ffn_b", 2 * i + (first_tile + n)),
                         scale=column("ffn_w", 6 * i + 3 * (first_tile + n))).then_inc(tap0_ready, 1)
                    if splits:
                        split(first_block // 2 + 2 * i + (n + 1), 1)
                    act.wait_ge(conv3_done, item)
                    copy(g_act[:, n], g_conv[:, n], ACT.Gelu_apprx_tanh).then_inc(gelu_ready, 1)
                    act.wait_ge(ft_ready, item)
                    copy(f_hi[:, 2 * i + (first_tile % F1 + n)], f_tmp[:, n], ACT.Copy).then_inc(f_hi_ready, 1)

                up(0, 0, B_UP1, 0, splits=False)
                split_block(B_UP1 + 6)
                up(0, 1, B_UP1, 0, splits=False)
                split_block(B_UP1 + 7)
                up(1, 0, B_UP1, 0, splits=False)
                up(1, 1, B_UP1, 0)
                with act.Fori(2, F1 // 2) as i:
                    for n in range(2):
                        up(i, n, B_UP1, 0)
                with act.Fori(0, KD_ // 2) as i:
                    for n in range(2):
                        split(B_DN1 // 2 + 2 * i + (n + 1), 0)
                        split(B_DN1 // 2 + 2 * i + (n + 1), 1)
                        copy(acc[:, 2 * i + n], ps[:, DN1_BANK + n], ACT.Copy).then_inc(d1_out, 1)
                for k in range(NP):
                    act.wait_ge(pt_done, c * NP + k + 1)
                    copy(f_hi[:, F1 - NP + k], ps[:, PV + k], ACT.Copy).then_inc(p_hi, 1)
                with act.Fori(0, F2 // 2) as i:
                    for n in range(2):
                        up(i, n, B_UP2, F1)
                nxt = B_DN2
                for j in range(KD_):
                    while nxt <= B_DN2 + (F2 * (j + 1) - 1) // 8:
                        split(nxt // 2 + 1, nxt % 2)
                        nxt += 1
                    act.wait_ge(d2_acc, c * KD_ + j + 1)
                    square(Q_PF + j, acc[:, j], j % 2)
                act.wait_ge(ssum_done, c * (NORMS - 1) + 4)
                root(ps[:, SMALL, 0:TT], D)
                for j in range(6):
                    if j == 0:
                        split(B_WP // 2 + 1, 0)
                    done(B_WP + j // 4)
                    copy(ple[:, j], ps[:, PLE_BANK[j]], ACT.Copy).then_inc(ple_out, 1)
                def h3_tiles(i):
                    for n in range(2):
                        act.wait_ge(h3_mid, c * KD_ + 2 * i + (n + 1))
                        copy(y_hi[:, 2 * i + n], h[:, 2 * i + n], ACT.Copy).then_inc(h3_hi, 1)

                h3_tiles(0)
                split(B_PG // 2, 1)
                h3_tiles(1)
                split(B_PG // 2 + 1, 0)
                h3_tiles(2)
                split(B_PG // 2 + 1, 1)
                h3_tiles(3)
                for j in range(6, KD_):
                    copy(ple[:, j], ps[:, PLE_BANK[j]], ACT.Copy).then_inc(ple_out, 1)

                def ple_gate(j):
                    done(B_PG + max(j, 3))
                    act.wait_ge(out_ready, c * KD_ + j + 1)
                    copy(ple_sg[:, j % 2], ps[:, PG_BANK[j]], ACT.Sigmoid).then_inc(ple_sig, 1)

                def out_rows(f):
                    act.wait_ge(ot_done, c * KD_ + f + 1)
                    copy(ple[:, f], ps[:, OT_BANK[f % 4]], ACT.Copy).then_inc(os_out, 1)
                    act.wait_ge(os_out, c * KD_ + f + 5)
                    act.dma_start(out[ds(c * T, T), P * f:P * f + P].rearrange("(t p) d -> p t d", p=P),
                                  four(ple[:, f])).then_inc(out_stored, 16)

                split(B_PG // 2 + 2, 0)
                split(B_PG // 2 + 2, 1)
                ple_gate(0)
                ple_gate(1)
                split(B_PG // 2 + 3, 0)
                ple_gate(2)
                ple_gate(3)
                split(B_PG // 2 + 3, 1)
                ple_gate(4)
                out_rows(0)
                ple_gate(5)
                out_rows(1)
                ple_gate(6)
                out_rows(2)
                out_rows(3)
                x_square(c + 1, 0)
                x_square(c + 1, 1)
                ple_gate(7)
                out_rows(4)
                out_rows(5)
                x_square(c + 1, 2)
                x_square(c + 1, 3)
                root(x_ss[:, :], D)
                out_rows(6)
                out_rows(7)
            act.wait_ge(out_stored, (CHUNKS + 1) * 16 * KD_)

        @block.tensor
        def _(pe):
            pe.sem_inc(block_done, SLOTS)
            pe.wait_ge(const_loaded, 32)
            pe.wait_ge(setup, SETUPS)
            with pe.Fori(0, CHUNKS) as c:
                def ready(b):
                    pe.wait_ge(w_lo_ready, c * NB + b + (1 + SLOTS))

                def product(bank, par, kk, hi, lo, start, stop):
                    nc.tensor.matmul(bank, w_hi[:, par, kk], hi, start=start, stop=False)
                    nc.tensor.matmul(bank, w_hi[:, par, kk], lo, start=False, stop=False)
                    return nc.tensor.matmul(bank, w_lo[:, par, kk], hi, start=False, stop=stop)

                def full_block(b, par, bank, hi, lo, between=None):
                    ready(b)
                    for k in range(8):
                        if k == 4 and between is not None:
                            between()
                        last = product(ps[:, bank], par, k, hi[:, k], lo[:, k], k == 0, k == 7)
                    last.then_inc(block_done, 1)

                def four_by_tile(b, banks, hi, lo, hi_there, lo_there):
                    for k in range(8):
                        if k % 2 == 0:
                            ready(b + k // 2)
                        pe.wait_ge(hi_there, c * KD_ + (k + 1))
                        par, first = k // 2 % 2, k % 2 * 4
                        for o in range(4):
                            nc.tensor.matmul(ps[:, banks[o]], w_hi[:, par, first + o], hi[:, k], start=(k == 0), stop=False)
                            nc.tensor.matmul(ps[:, banks[o]], w_lo[:, par, first + o], hi[:, k], start=False, stop=False)
                        pe.wait_ge(lo_there, c * KD_ + (k + 1))
                        for o in range(4):
                            last = nc.tensor.matmul(ps[:, banks[o]], w_hi[:, par, first + o], lo[:, k], start=False,
                                                    stop=(k == 7))
                        if k % 2 == 1:
                            last.then_inc(block_done, 1)

                def token_sums(n, q_end):
                    pe.wait_ge(ss_added, c * NQ + (q_end + 2))
                    for t in range(TT):
                        last = nc.tensor.matmul(ps[:, SMALL, t:t + 1], ssum[:, P * t:P * t + P], ones[:, 0:1],
                                                start=True, stop=True)
                    last.then_inc(ssum_done, 1)

                def spread(n):
                    pe.wait_ge(diag_ready, c * NORMS + (n + 1))
                    nc.tensor.matmul(ps[:, BC], ones[:, :], diag[:, :, :].rearrange("p t n -> p (t n)"),
                                     start=True, stop=True).then_inc(bc_ready, 1)

                pe.wait_ge(x_loaded, c * 16 + 16)
                pe.wait_ge(ple_sig, c * KD_ + 2)
                for f in range(KD_):
                    if f >= 4:
                        pe.wait_ge(h_loaded, c * KD_ + f - 3)
                    for t in range(TT):
                        last = nc.tensor.transpose(ps[:, XT_BANK + f % 4, P * t:P * t + P], x_rows[:, t, P * f:P * f + P], ident[:, :])
                    last.then_inc(xt_done, 1)
                pe.wait_ge(os_out, c * KD_ + 4)
                spread(N_X)
                pe.wait_ge(h_loaded, c * KD_ + KD_)
                four_by_tile(B_GLU, (0, 1, 2, 3), u_hi, u_lo, u_hi_ready, u_ready)
                for b in range(4, 8):
                    full_block(B_GLU + b, b % 2, b, u_hi, u_lo)
                for j in range(PAIRS + 1):
                    glu_tile = QK_BANK[j] // 2
                    pe.wait_ge(glu_done, c * NC + (glu_tile + 3))
                    full_block(B_QKV + j, j % 2, QK_BANK[j], u_hi, u_lo)
                ready(B_QKV + PAIRS + 1)
                for t in range(TT):
                    tok = slice(P * t, P * t + P)
                    for k in range(8):
                        nc.tensor.matmul(ps[:, V_BANK, tok], u_hi[:, k, tok], w_hi[:, 1, k], start=(k == 0), stop=False)
                        nc.tensor.matmul(ps[:, V_BANK, tok], u_lo[:, k, tok], w_hi[:, 1, k], start=False, stop=False)
                        last = nc.tensor.matmul(ps[:, V_BANK, tok], u_hi[:, k, tok], w_lo[:, 1, k], start=False, stop=(k == 7))
                last.then_inc(block_done, 1)
                pe.wait_ge(rope_done, c * (PAIRS + 1) + 4)

                def scores(i):
                    for s in range(2):
                        pe.wait_ge(q_diag_ready, c * SUB + 2 * i + (s + 1))
                        for a in range(PAIRS):
                            lhs = q_diag[:, s, a]
                            g = a // 2
                            if s == 0:
                                nc.tensor.matmul(ps[:, SC, P * a:P * a + CH], lhs, k_dup[:, g, ds(2 * CH * i + CH, CH)],
                                                 start=True, stop=True)
                                last = nc.tensor.matmul(ps[:, SC, P * a + CH:P * a + P], lhs, k_dup[:, g, ds(2 * CH * i, CH)],
                                                        start=True, stop=True)
                            else:
                                last = nc.tensor.matmul(ps[:, SC + 1, P * a:P * a + P], lhs,
                                                        k_dup[:, g, ds(2 * CH * i + CH, 2 * CH)], start=True, stop=True)
                        last.then_inc(qk_done, 1)

                def attend(i, more):
                    for n in range(2):
                        ready(B_GA + 2 * i + n)
                        pe.wait_ge(gate_a_ready, c * KD_ + 2 * i + (n + 1))
                        for k in range(8):
                            last = product(ps[:, GA_BANK + n], n, k, u_hi[:, k], u_lo[:, k], k == 0, k == 7)
                        last.then_inc(block_done, 1)
                    for s in range(2):
                        pe.wait_ge(pn_ready, c * SUB + 2 * i + (s + 1))
                        pe.wait_ge(ao_lo, c * SUB + 2 * i + (s + 1))
                        for a in range(PAIRS):
                            last = nc.tensor.transpose(ps[:, PV + s, P * a:P * a + P], prob[:, s, a], ident[:, :])
                        last.then_inc(t_done, 1)
                    if more:
                        scores(i + 1)
                    for s in range(2):
                        pe.wait_ge(pt_ready, c * SUB + 2 * i + (s + 1))
                        pe.wait_ge(v_cur_ready, c * SUB + 2 * i + (s + 1))
                        for a in range(PAIRS):
                            last = nc.tensor.matmul(ps[:, PV + s, P * a:P * a + P],
                                                    v_cur[:, s, a // 2].rearrange("p t d -> p (t d)"), probT[:, s, a],
                                                    start=True, stop=True)
                        last.then_inc(pv_done, 1)

                scores(0)
                with pe.Fori(0, SUB // 2 - 1) as i:
                    attend(i, True)
                attend(SUB // 2 - 1, False)

                def attention_outs(i, b, par):
                    ready(b)
                    for n in range(2):
                        pe.wait_ge(merged, c * KD_ + 2 * i + (n + 1))
                        for k in range(NC):
                            last = product(ps[:, AT_BANK[n]], par, NC * n + k, ca_hi[:, NC + k], ca_lo[:, NC + k],
                                           k == 0, k == NC - 1)
                    last.then_inc(block_done, 1)

                def conv_outs(i, b, par):
                    ready(b)
                    pe.wait_ge(merged, c * KD_ + 2 * i + 2)
                    for k in range(NC):
                        pe.wait_ge(c_lo, c * NC + (k + 1))
                        for n in range(2):
                            last = product(ps[:, CV_BANK[n]], par, 2 * k + n, ca_hi[:, k], ca_lo[:, k], k == 0, k == NC - 1)
                    last.then_inc(block_done, 1)

                def conv_mean():
                    pe.wait_ge(ao_lo, c * SUB + (SUB + 2))
                    pe.wait_ge(ln_summed, c * (NC - 1) + NC - 1)
                    nc.tensor.matmul(ps[:, BC], ones[:, :], ssum[:, :], start=True, stop=True).then_inc(mean_ready, 1)

                full_block(B_MRG, 0, GB_BANK[0], u_hi, u_lo)
                pe.wait_ge(gate_a_ready, c * KD_ + (KD_ + 2))
                full_block(B_MRG + 1, 1, GB_BANK[1], u_hi, u_lo, between=conv_mean)
                attention_outs(0, B_MRG + 2, 0)
                token_sums(N_LN, Q_LN + NC)
                pe.wait_ge(gate_b_ready, c * KD_ + 1)
                full_block(B_MRG + 3, 1, GB_BANK[0], u_hi, u_lo, between=lambda: spread(N_LN))
                conv_outs(0, B_MRG + 4, 0)
                pe.wait_ge(gate_b_ready, c * KD_ + 2)
                full_block(B_MRG + 5, 1, GB_BANK[1], u_hi, u_lo)
                attention_outs(1, B_MRG + 6, 0)
                conv_outs(1, B_MRG + 7, 1)
                with pe.Fori(2, KD_ // 2) as i:
                    for n in range(2):
                        pe.wait_ge(gate_b_ready, c * KD_ + 2 * i + (n - 1))
                        full_block(B_MRG + 4 * i + n, n, GB_BANK[n], u_hi, u_lo)
                    attention_outs(i, B_MRG + 4 * i + 2, 0)
                    conv_outs(i, B_MRG + 4 * i + 3, 1)
                pe.wait_ge(gate_b_ready, c * KD_ + KD_)
                four_by_tile(B_WO, WO_BANK[0:4], y_hi, y_lo, y_hi_ready, y_lo_ready)
                pe.wait_ge(merged, c * KD_ + (KD_ + 2))
                for j in range(4, KD_):
                    full_block(B_WO + j, j % 2, WO_BANK[j], y_hi, y_lo)
                pe.wait_ge(y2_out, c * KD_ + (4 + 4))
                token_sums(N_POST, Q_POST + KD_)
                spread(N_POST)
                pe.wait_ge(y2_out, c * KD_ + (KD_ + 4))
                four_by_tile(B_UP1, (0, 1, 2, 3), y_hi, y_lo, u2_hi, u2_lo)
                token_sums(N_PRE, Q_PRE + KD_)
                full_block(B_UP1 + 4, 0, 4, y_hi, y_lo, between=lambda: spread(N_PRE))
                full_block(B_UP1 + 5, 1, 5, y_hi, y_lo)

                def up_pair(i, n, first_block, first_tile):
                    pe.wait_ge(val_read, c * NF + 2 * i + (first_tile + n + 1))
                    for half in range(2):
                        full_block(first_block + 4 * i + 2 * n + half, half, 2 * n + half, y_hi, y_lo)

                up_pair(1, 1, B_UP1, 0)
                with pe.Fori(2, F1 // 2) as i:
                    for n in range(2):
                        up_pair(i, n, B_UP1, 0)
                with pe.Fori(0, KD_ // 2) as i:
                    for n in range(2):
                        pe.wait_ge(d1_out, c * KD_ + 2 * i + (n + 1))
                        for k in range(F1):
                            if k % 8 == 0:
                                ready(B_DN1 + 4 * i + 2 * n + k // 8)
                            pe.wait_ge(f_lo_ready, c * NF + (k + 1))
                            last = product(ps[:, DN1_BANK + n], k // 8, k % 8, f_hi[:, k], f_lo[:, k], k == 0, k == F1 - 1)
                            if k % 8 == 7:
                                last.then_inc(block_done, 1)
                pe.wait_ge(p_loaded, c * 16 + 16)
                for k in range(NP):
                    for t in range(TT):
                        last = nc.tensor.transpose(ps[:, PV + k, P * t:P * t + P], p_rows[:, t, P * k:P * k + P], ident[:, :])
                    last.then_inc(pt_done, 1)
                with pe.Fori(0, F2 // 2) as i:
                    for n in range(2):
                        up_pair(i, n, B_UP2, F1)
                pe.wait_ge(d1_out, c * KD_ + (KD_ + 2))
                for j in range(KD_):
                    if j == 2:
                        pe.wait_ge(val_read, c * NF + (NF + 2))
                    if j >= 4:
                        pe.wait_ge(d2_acc, c * KD_ + j - 3)
                    for k in range(F2):
                        q = F2 * j + k
                        if q % 8 == 0:
                            ready(B_DN2 + q // 8)
                        if j == 0:
                            pe.wait_ge(f_lo_ready, c * NF + (F1 + k + 1))
                        last = product(ps[:, DN2_BANK[j % 4]], q // 8 % 2, q % 8, f_hi[:, k], f_lo[:, k], k == 0, k == F2 - 1)
                        if q % 8 == 7:
                            last.then_inc(block_done, 1)

                def ple_out_tile(j):
                    if j == 0:
                        pe.wait_ge(p_lo, c * NP + NP)
                    if 2 <= j < 6:
                        pe.wait_ge(d2_acc, c * KD_ + j + 3)
                    if j >= 6:
                        pe.wait_ge(ple_out, c * KD_ + j - 5)
                    for k in range(NP):
                        q = NP * j + k
                        if q % 8 == 0:
                            ready(B_WP + q // 8)
                        last = product(ps[:, PLE_BANK[j]], q // 8, q % 8, f_hi[:, F1 - NP + k], f_lo[:, F1 - NP + k], k == 0, k == NP - 1)
                        if q % 8 == 7:
                            last.then_inc(block_done, 1)

                for j in range(6):
                    if j == 3:
                        token_sums(N_PF, Q_PF + KD_)
                    ple_out_tile(j)
                spread(N_PF)
                ple_out_tile(6)
                ple_out_tile(7)
                def out_tile(f):
                    pe.wait_ge(out_ready, c * KD_ + f + 3)
                    if f >= 4:
                        pe.wait_ge(os_out, c * KD_ + f + 1)
                    for t in range(TT):
                        last = nc.tensor.transpose(ps[:, OT_BANK[f % 4], P * t:P * t + P], h[:, f, P * t:P * t + P],
                                                   ident[:, :])
                    last.then_inc(ot_done, 1)

                pe.wait_ge(ple_out, c * KD_ + 6)
                four_by_tile(B_PG, PG_BANK[0:4], y_hi, y_lo, h3_hi, h3_lo)
                pe.wait_ge(ple_out, c * KD_ + KD_)
                full_block(B_PG + 4, 0, PG_BANK[4], y_hi, y_lo)
                full_block(B_PG + 5, 1, PG_BANK[5], y_hi, y_lo)
                out_tile(0)
                out_tile(1)
                pe.wait_ge(ple_sig, c * KD_ + (1 + 2))
                full_block(B_PG + 6, 0, PG_BANK[6], y_hi, y_lo)
                out_tile(2)
                out_tile(3)
                pe.wait_ge(ple_sig, c * KD_ + (2 + 2))
                full_block(B_PG + 7, 1, PG_BANK[7], y_hi, y_lo)
                for f in range(4, KD_):
                    out_tile(f)

        @block.vector
        def _(dve):
            V = nc.vector
            for s, n in ((glu_done, 2), (ao_lo, 2), (merged, 2), (val_read, 2), (ss_added, 2), (out_ready, 2)):
                dve.sem_inc(s, n)
            V.memset(ones[:, :], 1.0).then_inc(setup, 1)
            V.memset(prev_bias[:, :], -1e30).then_inc(setup, 1)
            V.memset(k_dup[:, :, :], 0.0).then_inc(setup, 1)
            V.memset(v_even[:, :, :], 0.0).then_inc(setup, 1)
            V.memset(conv_halo[:, :, :], 0.0).then_inc(setup, 1)
            V.memset(ffn_halo[:, :, :], 0.0).then_inc(setup, 1)
            V.memset(s_den[:, :, :], 0.0).then_inc(setup, 1)
            dve.wait_ge(const_loaded, 32)
            dve.wait_ge(setup, SETUPS)

            def norm(c, n, src, count):
                at = (c * NORMS + n) * 6
                dve.wait_ge(root_ready, c * NORMS + (n + 1))
                V.tensor_scalar(n_var[:, :], src, 1.0 / count, EPS, ALU.mult, ALU.add).then_inc(norm_step, 1)
                V.reciprocal(n_r[:, :], n_root[:, :]).then_inc(norm_step, 1)
                dve.wait_ge(norm_step, at + 2)
                V.tensor_tensor(n_t[:, :], n_r[:, :], n_r[:, :], ALU.mult).then_inc(norm_step, 1)
                dve.wait_ge(norm_step, at + 3)
                V.tensor_tensor(n_t[:, :], n_t[:, :], n_var[:, :], ALU.mult).then_inc(norm_step, 1)
                dve.wait_ge(norm_step, at + 4)
                V.tensor_scalar(n_t[:, :], n_t[:, :], -0.5, 1.5, ALU.mult, ALU.add).then_inc(norm_step, 1)
                dve.wait_ge(norm_step, at + 5)
                V.tensor_tensor(n_r[:, :], n_r[:, :], n_t[:, :], ALU.mult).then_inc(norm_step, 1)
                dve.wait_ge(norm_step, at + 6)
                V.tensor_tensor(diag[:, :, :], ident[:, :].unsqueeze(1).broadcast_to([P, TT, P]),
                                n_r[:, :].unsqueeze(2).broadcast_to([P, TT, P]), ALU.mult).then_inc(diag_ready, 1)

            def angles(c):
                dve.wait_ge(pos_loaded, c * 16 + 16)
                step = [0]

                def trig_link(ins):
                    step[0] += 1
                    ins.then_inc(trig_step, 1)
                    dve.wait_ge(trig_step, c * 14 + step[0])

                trig_link(V.tensor_copy(angle[:, :], pos_i[:, :]))
                trig_link(V.tensor_scalar(angle[:, :], angle[:, :], column("inv_freq"), None, ALU.mult))
                for s in range(2):
                    r = trig[:, s]
                    trig_link(V.tensor_scalar(turns[:, :], angle[:, :], float(1 / TWO_PI), 0.25 * s, ALU.mult, ALU.add))
                    trig_link(V.tensor_scalar(turns[:, :], turns[:, :], MAGIC, -MAGIC, ALU.add, ALU.add))
                    trig_link(V.scalar_tensor_tensor(r, turns[:, :], -C1, angle[:, :], ALU.mult, ALU.add))
                    trig_link(V.scalar_tensor_tensor(r, turns[:, :], -C2, r, ALU.mult, ALU.add))
                    trig_link(V.scalar_tensor_tensor(r, turns[:, :], -C3, r, ALU.mult, ALU.add))
                    trig_link(V.tensor_scalar(r, r, s * np.pi / 2, PI_IN, ALU.add, ALU.min))
                    V.tensor_scalar(r, r, -PI_IN, None, ALU.max).then_inc(trig_ready, 1)
                assert step[0] == 14

            angles(0)
            with dve.Fori(0, CHUNKS) as c:
                def done(b):
                    dve.wait_ge(block_done, c * NB + b + (1 + SLOTS))

                def zero_sum(which):
                    V.memset(ssum[:, :], 0.0).then_inc(ss_zeroed, 1)

                def add_square(q, slot, which):
                    dve.wait_ge(ss_zeroed, c * 4 + (which + 1))
                    dve.wait_ge(sq_ready, c * NQ + q + 1)
                    dve.wait_ge(ss_added, c * NQ + q + 2)
                    V.tensor_tensor(ssum[:, :], ssum[:, :], sq[:, slot], ALU.add).then_inc(ss_added, 1)

                def load_h(first, end):
                    for j in range(first, end):
                        dve.wait_ge(xt_done, c * KD_ + j + 1)
                        V.tensor_scalar(h[:, j], ps[:, XT_BANK + j % 4], 1.0, None, ALU.mult).then_inc(h_loaded, 1)

                load_h(0, 4)
                norm(c, N_X, x_ss[:, :], D)
                load_h(4, KD_)
                dve.wait_ge(bc_ready, c * NORMS + N_X + 1)
                for j in range(KD_ + 1):
                    if j < KD_:
                        dve.wait_ge(h_loaded, c * KD_ + j + 1)
                        if j >= 2:
                            dve.wait_ge(u_ready, c * KD_ + j - 1)
                        V.scalar_tensor_tensor(u_tmp[:, j % 2], h[:, j], column("g_pre_mix", j), ps[:, BC],
                                               ALU.mult, ALU.mult).then_inc(ut_ready, 1)
                    if j >= 1:
                        dve.wait_ge(u_hi_ready, c * KD_ + j)
                        V.tensor_tensor(u_lo[:, j - 1], u_tmp[:, (j - 1) % 2], u_hi[:, j - 1].bitcast(F32),
                                        ALU.subtract).then_inc(u_ready, 1)
                def tap(j, t, count, beside):
                    src = conv_in[:, j, ds(t, T)]
                    dst = conv_acc[:, j]
                    if isinstance(t, int) and t == 0:
                        V.tensor_scalar(dst, src, column("conv_w", j * TAPS), column("conv_b", j),
                                        ALU.mult, ALU.add).then_inc(conv_tap, 1)
                    else:
                        dve.wait_ge(conv_tap, c * (NC * TAPS) + (count - beside + 1))
                        V.scalar_tensor_tensor(dst, src, column("conv_w", t + j * TAPS), dst, ALU.mult,
                                               ALU.add).then_inc(conv_tap, 1)

                def early_taps(pair, first, end):
                    for t in range(first, end):
                        for n in range(2):
                            tap(2 * pair + n, t, 2 * (pair * EARLY + t) + n, 2)

                def glu(pair):
                    for j in (2 * pair, 2 * pair + 1):
                        dve.wait_ge(glu_sig, c * NC + j + 1)
                        V.tensor_tensor(conv_in[:, j, HALO:], ps[:, 2 * j], glu_sg[:, j % 2], ALU.mult).then_inc(glu_done, 1)
                    dve.wait_ge(glu_done, c * NC + 2 * pair + 4)

                dve.wait_ge(glu_sig, c * NC + 1)
                V.tensor_copy(conv_in[:, :, 0:HALO], conv_halo[:, :, :]).then_inc(halo_in, 1)
                dve.wait_ge(halo_in, c + 1)
                glu(0)
                early_taps(0, 0, EARLY)
                glu(1)
                V.tensor_copy(conv_halo[:, :, :], conv_in[:, :, T:])
                dve.wait_ge(trig_done, c * 2 + 2)
                V.tensor_copy(k_dup[:, :, 0:CH], k_dup[:, :, T:T + CH]).then_inc(k_halo, 1)
                dve.wait_ge(k_halo, c + 1)
                for j in range(PAIRS + 1):
                    early_taps(1, min(EARLY, 4 * j), min(EARLY, 4 * j + 4))
                    if j == PAIRS:
                        V.memset(q_diag[:, :, :, :], 0.0).then_inc(q_zeroed, 1)
                    at = (c * (PAIRS + 1) + j) * 2
                    done(B_QKV + j)
                    dve.wait_ge(rope_swapped, c * (PAIRS + 1) + j + 1)
                    V.tensor_tensor(rope_a[:, j % 2], ps[:, QK_BANK[j]], cos_t[:, :], ALU.mult).then_inc(rope_step, 1)
                    V.tensor_tensor(rope_b[:, j % 2], rope_b[:, j % 2], sin_t[:, :], ALU.mult).then_inc(rope_step, 1)
                    dve.wait_ge(rope_step, at + 2)
                    if j < PAIRS:
                        V.tensor_tensor(qT[:, j], rope_a[:, j % 2], rope_b[:, j % 2], ALU.add).then_inc(rope_done, 1)
                    else:
                        for g in range(2):
                            for to in range(2):
                                last = V.tensor_tensor(k_dup[CH * to:CH * to + CH, g, CH:], rope_a[CH * g:CH * g + CH, j % 2],
                                                       rope_b[CH * g:CH * g + CH, j % 2], ALU.add)
                        last.then_inc(rope_done, 1)
                    dve.wait_ge(rope_done, c * (PAIRS + 1) + j + 1)
                def score_maxima(i):
                    first = isinstance(i, int)
                    step = [0 if first else 1]

                    def link(ins):
                        step[0] += 1
                        ins.then_inc(sm_step, 1)
                        dve.wait_ge(sm_step, c * (SUB // 2 * 4 + 1) + i * 4 + step[0])

                    for s in range(2):
                        scores = four(ps[:, SC + s])
                        dve.wait_ge(qk_done, c * SUB + 2 * i + (s + 1))
                        if s == 0 and first:
                            link(V.tensor_tensor(scores[:, :, CH:], scores[:, :, CH:],
                                                 prev_bias[:, :].unsqueeze(1).broadcast_to([P, PAIRS, CH]), ALU.add))
                            V.memset(prev_bias[:, :], 0.0)
                        link(V.tensor_reduce(s_max[:, s], scores, AX.X, ALU.max))
                        link(V.scalar_tensor_tensor(s_m[:, s], s_max[:, s], SCALE, column_range("sinks"), ALU.mult, ALU.max))
                        V.tensor_tensor(s_sink[:, s], column_range("sinks"), s_m[:, s], ALU.subtract)
                        V.tensor_scalar(s_neg[:, s], s_m[:, s], -1.0, None, ALU.mult).then_inc(sm_ready, 1)

                def attend(i, more):
                    step = [0]

                    def link(ins):
                        step[0] += 1
                        ins.then_inc(pn_step, 1)
                        dve.wait_ge(pn_step, c * (SUB // 2 * 4) + i * 4 + step[0])

                    def taps(first, end):
                        for n in range(first, end):
                            tap(n % NC, i * (LATE // NC) + (EARLY + n // NC), i * LATE + (NC * EARLY + n), NC)

                    for s in range(2):
                        dve.wait_ge(exp_done, c * SUB + 2 * i + (s + 1))
                        link(V.tensor_tensor(s_den[:, s], s_den[:, s], s_sinke[:, s], ALU.add))
                        link(V.reciprocal(s_rec[:, s], s_den[:, s]))
                        V.tensor_tensor(prob[:, s], prob[:, s], s_rec[:, s].unsqueeze(2).broadcast_to([P, PAIRS, P]),
                                        ALU.mult).then_inc(pn_ready, 1)
                    taps(0, TAPS_A if more else LATE)
                    if more:
                        score_maxima(i + 1)
                        taps(TAPS_A, TAPS_B)
                    for s in range(2):
                        dve.wait_ge(ao_hi, c * SUB + 2 * i + (s + 1))
                        now = ds(2 * CH * i + CH * s, CH)
                        ao = four(ps[:, PV + s])
                        V.tensor_tensor(ca_lo[0:CH, NC:, now], ao[0:CH, :, 0:CH], ca_hi[0:CH, NC:, now].bitcast(F32), ALU.subtract)
                        V.tensor_tensor(ca_lo[CH:P, NC:, now], ao[CH:P, :, CH:P], ca_hi[CH:P, NC:, now].bitcast(F32),
                                        ALU.subtract).then_inc(ao_lo, 1)
                    if more:
                        taps(TAPS_B, LATE)
                        dve.wait_ge(conv_tap, c * (NC * TAPS) + NC * EARLY + i * LATE + LATE)

                score_maxima(0)
                with dve.Fori(0, SUB // 2 - 1) as i:
                    attend(i, True)
                attend(SUB // 2 - 1, False)
                dve.wait_ge(conv_tap, c * (NC * TAPS) + NC * TAPS)
                for j in range(1, NC):
                    V.tensor_tensor(ssum[:, :], conv_acc[:, 0] if j == 1 else ssum[:, :], conv_acc[:, j], ALU.add).then_inc(ln_summed, 1)
                    dve.wait_ge(ln_summed, c * (NC - 1) + j)
                dve.wait_ge(mean_ready, c + 1)
                for j in range(NC):
                    V.scalar_tensor_tensor(conv_acc[:, j], ps[:, BC], -1.0 / CONV, conv_acc[:, j], ALU.mult,
                                           ALU.add).then_inc(ln_centred, 1)
                zero_sum(0)
                for j in range(NC):
                    add_square(Q_LN + j, j % 2, 0)
                norm(c, N_LN, ps[:, SMALL, 0:TT], CONV)
                dve.wait_ge(bc_ready, c * NORMS + N_LN + 1)
                for j in range(NC + 2):
                    if j < NC:
                        V.scalar_tensor_tensor(conv_acc[:, j], conv_acc[:, j], column("ln_g", j), ps[:, BC], ALU.mult,
                                               ALU.mult).then_inc(ln_scaled, 1)
                    if j >= 2:
                        dve.wait_ge(c_hi, c * NC + j - 1)
                        V.tensor_tensor(ca_lo[:, j - 2], silu_c[:, j % 2], ca_hi[:, j - 2].bitcast(F32),
                                        ALU.subtract).then_inc(c_lo, 1)
                with dve.Fori(0, KD_ // 2) as i:
                    done(B_MRG + 4)
                    done(B_MRG + 4 * i + 3)
                    for n in range(2):
                        item = c * KD_ + 2 * i + (n + 1)
                        V.tensor_tensor(part_a[:, n], ps[:, CV_BANK[n]], gate_a[:, 2 * i + n], ALU.mult).then_inc(part_a_ready, 1)
                        dve.wait_ge(gate_b_ready, item)
                        V.tensor_tensor(part_b[:, n], ps[:, AT_BANK[n]], gate_b[:, n], ALU.mult).then_inc(merged, 1)
                        dve.wait_ge(part_a_ready, item)
                        dve.wait_ge(merged, item + 2)
                        V.tensor_tensor(y_tmp[:, n], part_a[:, n], part_b[:, n], ALU.add).then_inc(yt_ready, 1)
                        dve.wait_ge(y_hi_ready, item)
                        V.tensor_tensor(y_lo[:, 2 * i + n], y_tmp[:, n], y_hi[:, 2 * i + n].bitcast(F32),
                                        ALU.subtract).then_inc(y_lo_ready, 1)
                    dve.wait_ge(y_lo_ready, c * KD_ + 2 * i + 2)
                zero_sum(1)
                with dve.Fori(0, KD_ // 2) as i:
                    for n in range(2):
                        add_square(Q_POST + 2 * i + n, n, 1)
                    dve.wait_ge(ss_added, c * NQ + 2 * i + (Q_POST + 4))
                norm(c, N_POST, ps[:, SMALL, 0:TT], D)
                zero_sum(2)
                dve.wait_ge(bc_ready, c * NORMS + N_POST + 1)

                def normed(j, gain, step):
                    V.scalar_tensor_tensor(h_tmp[:, j % 2], acc[:, j], column(gain, j), ps[:, BC],
                                           ALU.mult, ALU.mult).then_inc(step, 1)

                def residual(j, step, there):
                    dve.wait_ge(step, c * KD_ + j + 1)
                    V.tensor_tensor(h[:, j], h[:, j], h_tmp[:, j % 2], ALU.add).then_inc(there, 1)

                normed(0, "g_post_mix", mid_step)
                for j in range(KD_ + 2):
                    if j == 0:
                        residual(0, mid_step, h_mid)
                        normed(1, "g_post_mix", mid_step)
                        continue
                    if j + 1 < KD_:
                        dve.wait_ge(h_mid, c * KD_ + j)
                        normed(j + 1, "g_post_mix", mid_step)
                    if j < KD_:
                        residual(j, mid_step, h_mid)
                    if 1 <= j <= KD_:
                        dve.wait_ge(u2_hi, c * KD_ + j)
                        V.scalar_tensor_tensor(y_lo[:, j - 1], h[:, j - 1], column("g_pre_ffn", j - 1),
                                               y_hi[:, j - 1].bitcast(F32), ALU.mult, ALU.subtract).then_inc(u2_lo, 1)
                    if j >= 2:
                        add_square(Q_PRE + j - 2, j % 2, 2)
                norm(c, N_PRE, ps[:, SMALL, 0:TT], D)

                def up(i, first_block, first_tile, banks=(0, 2)):
                    together = first_tile == 0 and isinstance(i, int) and i == 0
                    if not together:
                        dve.wait_ge(f_lo_ready, c * NF + 2 * i + first_tile)
                    for n in range(2):
                        item = c * NF + 2 * i + (first_tile + n + 1)
                        at = (c * NF + 2 * i + (first_tile + n)) * 3
                        halo = ffn_halo[:, 2 * i + (first_tile + n)]
                        slot = 2 * i + (first_tile % F1 + n)

                        def value():
                            done(first_block + (3 if together else 4 * i + 2 * n + 1))
                            V.tensor_tensor(f_val[:, n], ps[:, banks[n] + 1], r_ffn[:, :], ALU.mult).then_inc(val_read, 1)

                        done(first_block + (3 if together else 4 * i + 2 * n))
                        V.tensor_copy(g_in[:, n, 0:2], halo).then_inc(ffn_step, 1)
                        V.tensor_tensor(g_in[:, n, 2:], ps[:, banks[n]], r_ffn[:, :], ALU.mult).then_inc(ffn_step, 1)
                        dve.wait_ge(ffn_step, at + 2)
                        V.tensor_scalar(halo, g_in[:, n, T:], 1.0, None, ALU.mult).then_inc(g_in_ready, 1)
                        if together:
                            value()
                        dve.wait_ge(tap0_ready, item)
                        V.scalar_tensor_tensor(g_conv[:, n], g_in[:, n, 1:T + 1], column("ffn_w", 6 * i + (3 * (first_tile + n) + 1)),
                                               g_conv[:, n], ALU.mult, ALU.add).then_inc(ffn_step, 1)
                        dve.wait_ge(ffn_step, at + 3)
                        V.scalar_tensor_tensor(g_conv[:, n], g_in[:, n, 2:], column("ffn_w", 6 * i + (3 * (first_tile + n) + 2)),
                                               g_conv[:, n], ALU.mult, ALU.add).then_inc(conv3_done, 1)
                        if not together:
                            value()
                        dve.wait_ge(val_read, item + 2)
                        dve.wait_ge(gelu_ready, item)
                        V.tensor_tensor(f_tmp[:, n], g_act[:, n], f_val[:, n], ALU.mult).then_inc(ft_ready, 1)
                        dve.wait_ge(f_hi_ready, item)
                        V.tensor_tensor(f_lo[:, slot], f_tmp[:, n], f_hi[:, slot].bitcast(F32),
                                        ALU.subtract).then_inc(f_lo_ready, 1)

                dve.wait_ge(r_ffn_ready, c + 1)
                up(0, B_UP1, 0)
                up(1, B_UP1, 0, banks=(4, 2))
                with dve.Fori(2, F1 // 2) as i:
                    up(i, B_UP1, 0)
                for k in range(NP):
                    dve.wait_ge(p_hi, c * NP + k + 1)
                    V.tensor_tensor(f_lo[:, F1 - NP + k], ps[:, PV + k], f_hi[:, F1 - NP + k].bitcast(F32),
                                    ALU.subtract).then_inc(p_lo, 1)
                with dve.Fori(0, F2 // 2) as i:
                    up(i, B_UP2, F1)
                zero_sum(3)
                for j in range(KD_):
                    done(B_DN2 + (F2 * (j + 1) - 1) // 8)
                    V.tensor_tensor(acc[:, j], acc[:, j], ps[:, DN2_BANK[j % 4]], ALU.add).then_inc(d2_acc, 1)
                    if j >= 1:
                        add_square(Q_PF + j - 1, (j - 1) % 2, 3)
                add_square(Q_PF + KD_ - 1, (KD_ - 1) % 2, 3)
                norm(c, N_PF, ps[:, SMALL, 0:TT], D)
                dve.wait_ge(bc_ready, c * NORMS + N_PF + 1)
                normed(0, "g_post_ffn", h3_step)
                for j in range(KD_ + 1):
                    if j == 0:
                        residual(0, h3_step, h3_mid)
                        normed(1, "g_post_ffn", h3_step)
                        continue
                    if j + 1 < KD_:
                        dve.wait_ge(h3_mid, c * KD_ + j)
                        normed(j + 1, "g_post_ffn", h3_step)
                    if j < KD_:
                        residual(j, h3_step, h3_mid)
                    if j >= 1:
                        dve.wait_ge(h3_hi, c * KD_ + j)
                        V.tensor_tensor(y_lo[:, j - 1], h[:, j - 1], y_hi[:, j - 1].bitcast(F32),
                                        ALU.subtract).then_inc(h3_lo, 1)
                angles(c + 1)
                with dve.Fori(0, KD_ // 2) as i:
                    dve.wait_ge(ple_out, c * KD_ + KD_)
                    for n in range(2):
                        item = c * KD_ + 2 * i + (n + 1)
                        dve.wait_ge(ple_sig, item + 2)
                        V.tensor_tensor(ple_t[:, n], ple[:, 2 * i + n], ple_sg[:, n], ALU.mult).then_inc(ple_mul, 1)
                        dve.wait_ge(ple_mul, item)
                        V.tensor_tensor(h[:, 2 * i + n], h[:, 2 * i + n], ple_t[:, n], ALU.add).then_inc(out_ready, 1)
                    dve.wait_ge(out_ready, c * KD_ + 2 * i + 4)
            dve.wait_ge(root_ready, CHUNKS * NORMS + 1)



def _tiles(w, rows, cols):
    return [w[r * P:(r + 1) * P, n * P:(n + 1) * P] for r, n in zip(rows, cols)]


def weight_stream(w_in, w_conv_out, w_attn_out, w_out, w_up, w_down, w_ple, w_ple_gate):
    tiles = []

    def column_of(w, n, rows=None):
        tiles.extend(_tiles(w, rows or range(w.shape[0] // P), [n] * (len(rows) if rows else w.shape[0] // P)))

    def four_by_tile(w, columns):
        for k in range(8):
            for n in columns:
                tiles.extend(_tiles(w, [k], [n]))

    def pairs(w, js, second):
        for j in js:
            column_of(w, j)
            column_of(w, second + j)

    four_by_tile(w_in, (0, NC, 1, NC + 1))
    pairs(w_in, range(2, NC), NC)
    first = 2 * NC
    for j in range(PAIRS + 2):
        column_of(w_in, first + j)
    first += PAIRS + 2
    for j in range(KD_):
        column_of(w_in, first + j)
    for j in range(0, KD_, 2):
        column_of(w_in, first + KD_ + j)
        column_of(w_in, first + KD_ + j + 1)
        column_of(w_attn_out, j)
        column_of(w_attn_out, j + 1)
        for k in range(NC):
            tiles.extend(_tiles(w_conv_out, [k, k], [j, j + 1]))
    first = 8 * (B_MRG + 3)
    conv_outs, gate_b = tiles[first:first + 8], tiles[first + 8:first + 16]
    tiles[first:first + 16] = gate_b + conv_outs
    four_by_tile(w_out, range(4))
    for j in range(4, KD_):
        column_of(w_out, j)
    four_by_tile(w_up, (0, NF, 1, NF + 1))
    pairs(w_up, range(2, F1), NF)
    for j in range(KD_):
        column_of(w_down, j, list(range(F1)))
    pairs(w_up, range(F1, NF), NF)
    for j in range(KD_):
        column_of(w_down, j, list(range(F1, NF)))
    for j in range(KD_):
        column_of(w_ple, j)
    four_by_tile(w_ple_gate, range(4))
    for j in range(4, KD_):
        column_of(w_ple_gate, j)
    stream = np.stack(tiles).reshape(NB, 8, P, P)
    return np.ascontiguousarray(stream.transpose(0, 2, 1, 3)).reshape(NB, P, 8 * P)


def column_array(g_pre_mix, conv_dw_w, conv_dw_b, conv_ln_g, conv_ln_b, g_post_mix, g_pre_ffn, ffn_dw_w, ffn_dw_b,
                 g_post_ffn, attn_sinks):
    def cols(v):
        return v.reshape(-1, P).T

    def taps(w):
        return w.T.reshape(-1, P, w.shape[0]).transpose(1, 0, 2).reshape(P, -1)

    half = HD // 2
    inv_freq = (10000.0 ** (-np.arange(half) / half)).astype(np.float32)
    sign = np.where(np.arange(P) % HD < half, -1.0, 1.0).astype(np.float32)
    parts = {
        "g_pre_mix": cols(g_pre_mix), "conv_w": taps(conv_dw_w), "conv_b": cols(conv_dw_b), "ln_g": cols(conv_ln_g),
        "ln_b": cols(conv_ln_b), "g_post_mix": cols(g_post_mix), "g_pre_ffn": cols(g_pre_ffn), "ffn_w": taps(ffn_dw_w),
        "ffn_b": cols(ffn_dw_b), "g_post_ffn": cols(g_post_ffn),
        "sinks": np.repeat(attn_sinks.reshape(PAIRS, 2).T, CH, axis=0),
        "inv_freq": np.tile(inv_freq, P // half)[:, None], "sin_sign": sign[:, None],
        "eps": np.full((P, 1), EPS, np.float32),
    }
    return np.ascontiguousarray(np.concatenate([parts[n] for n in COLS], axis=1))


def kernel(x, p, positions, g_pre_mix, w_in, conv_dw_w, conv_dw_b, conv_ln_g, conv_ln_b, w_conv_out, attn_sinks,
           w_attn_out, w_out, g_post_mix, g_pre_ffn, w_up, ffn_dw_w, ffn_dw_b, w_down, g_post_ffn, w_ple, w_ple_gate):
    import concourse.bacc as bacc
    from concourse.bass_utils import run_bass_kernel_spmd

    n = {k: np.asarray(v) for k, v in locals().items() if k not in ("bacc", "run_bass_kernel_spmd")}
    arrays = {
        "x": np.ascontiguousarray(n["x"][0]),
        "p": np.ascontiguousarray(n["p"][0, 0]),
        "positions": np.ascontiguousarray(n["positions"]),
        "weights": weight_stream(*(n[k][0] for k in ("w_in", "w_conv_out", "w_attn_out", "w_out", "w_up", "w_down",
                                                     "w_ple", "w_ple_gate"))),
        "columns": column_array(*(n[k][0] for k in ("g_pre_mix", "conv_dw_w", "conv_dw_b", "conv_ln_g", "conv_ln_b",
                                                    "g_post_mix", "g_pre_ffn", "ffn_dw_w", "ffn_dw_b", "g_post_ffn",
                                                    "attn_sinks"))),
        "identity": np.eye(P, dtype=np.float32),
    }
    nc = bacc.Bacc("TRN2", target_bir_lowering=False, num_devices=1, dynamic_dma_scratch_size=1024)
    args = {k: nc.dram_tensor(f"in_{k}", a.shape, mybir.dt.from_np(a.dtype), kind="ExternalInput").ap()
            for k, a in arrays.items()}
    out = nc.dram_tensor("out_h", (SEQ, D), F32, kind="ExternalOutput").ap()
    build_kernel(nc, out=out, **args)
    got = run_bass_kernel_spmd(nc, [{f"in_{k}": a for k, a in arrays.items()}], core_ids=[0])
    return got.results[0]["out_h"].reshape(1, SEQ, D)
```
